# Optimizing a Trainium2 kernel written in Bass

```python
import jax, jax.numpy as jnp
from jax import lax
import numpy as np

D_MODEL = 1024
BATCH = 1
SEQ = 256
DEPTH = 2

HG_HEADS = 4
HG_DK = 64
HG_DV = 64
HG_CHUNK = 64
MLA_HEADS = 4
MLA_Q_RANK = 256
MLA_KV_RANK = 128
MLA_NOPE = 64
MLA_ROPE = 32
MLA_V = 64
MLA_QK = MLA_NOPE + MLA_ROPE
ROPE_BASE = 10000.0
CONV_CH = 256
CONV_K = 31
SB_HEADS = 4
SB_HEAD_DIM = 64
N_BRANCH = 4
BRANCH_W = 256
D_FF = 2816
FFN_CONV_K = 3
ATTN_BLOCK = 128
EPS = 1e-6

IN_COLS = (HG_HEADS * HG_DK, HG_HEADS * HG_DK, HG_HEADS * HG_DV, HG_HEADS * HG_DV,
           MLA_Q_RANK, MLA_KV_RANK, MLA_ROPE,
           2 * CONV_CH,
           SB_HEADS * SB_HEAD_DIM, SB_HEADS * SB_HEAD_DIM, SB_HEADS * SB_HEAD_DIM,
           N_BRANCH * D_MODEL)
D_IN = 4 * 256 + 256 + 128 + 32 + 512 + 3 * 256 + 4 * 1024

kernel_name = "hybrid_gated_parallel_mixer_block"

F32 = jnp.float32

def _rmsnorm(x, g):
    xf = x.astype(F32)
    y = xf * lax.rsqrt(jnp.mean(xf * xf, axis=-1, keepdims=True) + EPS)
    return (y * g.astype(F32)).astype(x.dtype)

def _layernorm(x, g, b):
    xf = x.astype(F32)
    xc = xf - jnp.mean(xf, axis=-1, keepdims=True)
    var = jnp.mean(xc * xc, axis=-1, keepdims=True)
    return (xc * lax.rsqrt(var + 1e-5) * g.astype(F32) + b.astype(F32)).astype(x.dtype)

def _causal_dwconv(u, w, b):
    k, c = w.shape
    out = lax.conv_general_dilated(
        u, w[:, None, :].astype(u.dtype), window_strides=(1,), padding=[(k - 1, 0)],
        dimension_numbers=('NWC', 'WIO', 'NWC'), feature_group_count=c)
    return out + b.astype(u.dtype)

def _rotary(x, pos):
    half = x.shape[-1] // 2
    freqs = ROPE_BASE ** (-jnp.arange(half, dtype=F32) / half)
    ang = pos.astype(F32)[:, None] * freqs[None, :]
    cos = jnp.cos(ang)[None, :, None, :]
    sin = jnp.sin(ang)[None, :, None, :]
    xf = x.astype(F32)
    x1, x2 = xf[..., :half], xf[..., half:]
    return jnp.concatenate([x1 * cos - x2 * sin, x2 * cos + x1 * sin], axis=-1).astype(x.dtype)

def _to_blocks(t, size):
    b, h, s, d = t.shape
    return t.reshape(b, h, s // size, size, d).transpose(2, 0, 1, 3, 4)

def _from_blocks(t):
    nb, b, h, size, d = t.shape
    return t.transpose(1, 2, 0, 3, 4).reshape(b, h, nb * size, d)

def _chunk_gated_recurrence(q, k, v, log_f):
    b_, h_, _, dk = q.shape
    dv = v.shape[-1]
    causal = jnp.tril(jnp.ones((HG_CHUNK, HG_CHUNK), dtype=bool))

    def step(state, inp):
        qc, kc, vc, lfc = inp
        bcum = jnp.cumsum(lfc, axis=2)
        o_inter = jnp.einsum('bhtk,bhkv->bhtv', qc * jnp.exp(bcum), state)
        diff = jnp.where(causal[:, :, None],
                         bcum[:, :, :, None, :] - bcum[:, :, None, :, :], -jnp.inf)
        a = jnp.einsum('bhtk,bhsk,bhtsk->bhts', qc, kc, jnp.exp(diff))
        o_intra = jnp.einsum('bhts,bhsv->bhtv', a, vc)
        b_last = bcum[:, :, -1:, :]
        new_state = (jnp.exp(b_last[:, :, 0, :])[..., None] * state
                     + jnp.einsum('bhsk,bhsv->bhkv', kc * jnp.exp(b_last - bcum), vc))
        return new_state, o_inter + o_intra

    s0 = jnp.zeros((b_, h_, dk, dv), F32)
    xs = (_to_blocks(q, HG_CHUNK), _to_blocks(k, HG_CHUNK),
          _to_blocks(v, HG_CHUNK), _to_blocks(log_f, HG_CHUNK))
    _, o = lax.scan(step, s0, xs)
    return _from_blocks(o)

def _causal_softmax_attn(q, k, v, scale):
    s = q.shape[2]
    kpos = jnp.arange(s)

    def one(args):
        qi, i = args
        sc = jnp.einsum('bhtd,bhsd->bhts', qi, k).astype(F32) * scale
        qpos = i * ATTN_BLOCK + jnp.arange(ATTN_BLOCK)
        sc = jnp.where(kpos[None, :] <= qpos[:, None], sc, -jnp.inf)
        p = jax.nn.softmax(sc, axis=-1)
        return jnp.einsum('bhts,bhsv->bhtv', p.astype(v.dtype), v)

    out = lax.map(one, (_to_blocks(q, ATTN_BLOCK), jnp.arange(s // ATTN_BLOCK)))
    return _from_blocks(out)

def _stick_breaking_attn(q, k, v, scale):
    s = q.shape[2]
    kpos = jnp.arange(s)

    def one(args):
        qi, i = args
        z = jnp.einsum('bhtd,bhsd->bhts', qi, k).astype(F32) * scale
        qpos = i * ATTN_BLOCK + jnp.arange(ATTN_BLOCK)
        mask = kpos[None, :] < qpos[:, None]
        log_beta = jax.nn.log_sigmoid(z)
        log_1mb = jnp.where(mask, jax.nn.log_sigmoid(-z), 0.0)
        after = lax.cumsum(log_1mb, axis=3, reverse=True) - log_1mb
        w = jnp.where(mask, jnp.exp(log_beta + after), 0.0)
        return jnp.einsum('bhts,bhsv->bhtv', w.astype(v.dtype), v)

    out = lax.map(one, (_to_blocks(q, ATTN_BLOCK), jnp.arange(s // ATTN_BLOCK)))
    return _from_blocks(out)

def _heads(t, n, d):
    b, s, _ = t.shape
    return t.reshape(b, s, n, d).transpose(0, 2, 1, 3)

def _hgrn2_branch(hq, hf, hv, hg, lb, g_out):
    b, s, _ = hq.shape
    lb = lb.astype(F32)
    ff = hf.astype(F32)
    q = jax.nn.silu(hq.astype(F32))
    log_f = jnp.logaddexp(jnp.log(lb), jnp.log1p(-lb) + jax.nn.log_sigmoid(ff))
    k = (1.0 - lb) * jax.nn.sigmoid(-ff)
    o = _chunk_gated_recurrence(_heads(q, HG_HEADS, HG_DK), _heads(k, HG_HEADS, HG_DK),
                                _heads(hv.astype(F32), HG_HEADS, HG_DV),
                                _heads(log_f, HG_HEADS, HG_DK))
    o = _rmsnorm(o.transpose(0, 2, 1, 3), g_out)
    o = o * jax.nn.silu(hg.astype(F32)).reshape(b, s, HG_HEADS, HG_DV)
    return o.reshape(b, s, HG_HEADS * HG_DV).astype(hq.dtype)

def _mla_branch(cq, ckv, kr, g_q_lat, w_uq, g_kv_lat, w_ukv, g_qk_q, g_qk_k, pos):
    b, s, _ = cq.shape
    q = (_rmsnorm(cq, g_q_lat) @ w_uq).reshape(b, s, MLA_HEADS, MLA_QK)
    kv = (_rmsnorm(ckv, g_kv_lat) @ w_ukv).reshape(b, s, MLA_HEADS, MLA_NOPE + MLA_V)
    k_nope, v = kv[..., :MLA_NOPE], kv[..., MLA_NOPE:]
    k_rope = jnp.broadcast_to(kr[:, :, None, :], (b, s, MLA_HEADS, MLA_ROPE))
    k = jnp.concatenate([k_nope, k_rope], axis=-1)
    q = _rmsnorm(q, g_qk_q)
    k = _rmsnorm(k, g_qk_k)
    q = jnp.concatenate([q[..., :MLA_NOPE], _rotary(q[..., MLA_NOPE:], pos)], axis=-1)
    k = jnp.concatenate([k[..., :MLA_NOPE], _rotary(k[..., MLA_NOPE:], pos)], axis=-1)
    o = _causal_softmax_attn(q.transpose(0, 2, 1, 3), k.transpose(0, 2, 1, 3),
                             v.transpose(0, 2, 1, 3), MLA_QK ** -0.5)
    return o.transpose(0, 2, 1, 3).reshape(b, s, MLA_HEADS * MLA_V)

def _conformer_conv_branch(cu, conv_w, conv_b, ln_g, ln_b):
    a, g = jnp.split(cu, 2, axis=-1)
    u = a * jax.nn.sigmoid(g)
    u = _causal_dwconv(u, conv_w, conv_b)
    u = _layernorm(u, ln_g, ln_b)
    return jax.nn.silu(u)

def _stick_breaking_branch(sq, sk, sv):
    b, s, _ = sq.shape
    o = _stick_breaking_attn(_heads(sq, SB_HEADS, SB_HEAD_DIM), _heads(sk, SB_HEADS, SB_HEAD_DIM),
                             _heads(sv, SB_HEADS, SB_HEAD_DIM), SB_HEAD_DIM ** -0.5)
    return o.transpose(0, 2, 1, 3).reshape(b, s, SB_HEADS * SB_HEAD_DIM)

def setup_inputs(seed: int = 0) -> dict:
    key = jax.random.key(seed)
    ks = jax.random.split(key, 24)

    def nrm(k, shape, scale):
        return jax.random.normal(k, shape, F32) * scale

    def gain(k, shape):
        return 1.0 + 0.1 * jax.random.normal(k, shape, F32)

    res_scale = (2.0 * DEPTH) ** -0.5
    L = DEPTH
    return {
        "x": nrm(ks[0], (BATCH, SEQ, D_MODEL), 1.0),
        "g_mix": gain(ks[1], (L, D_MODEL)),
        "w_in": nrm(ks[2], (L, D_MODEL, D_IN), D_MODEL ** -0.5),
        "lb_logits": nrm(ks[3], (L, HG_HEADS * HG_DK), 0.5),
        "g_hg_out": gain(ks[4], (L, HG_DV)),
        "g_q_lat": gain(ks[5], (L, MLA_Q_RANK)),
        "w_uq": nrm(ks[6], (L, MLA_Q_RANK, MLA_HEADS * MLA_QK), MLA_Q_RANK ** -0.5),
        "g_kv_lat": gain(ks[7], (L, MLA_KV_RANK)),
        "w_ukv": nrm(ks[8], (L, MLA_KV_RANK, MLA_HEADS * (MLA_NOPE + MLA_V)), MLA_KV_RANK ** -0.5),
        "g_qk_q": gain(ks[9], (L, MLA_QK)),
        "g_qk_k": gain(ks[10], (L, MLA_QK)),
        "conv_w": nrm(ks[11], (L, CONV_K, CONV_CH), CONV_K ** -0.5),
        "conv_b": nrm(ks[12], (L, CONV_CH), 0.02),
        "conv_ln_g": gain(ks[13], (L, CONV_CH)),
        "conv_ln_b": nrm(ks[14], (L, CONV_CH), 0.02),
        "w_branch": nrm(ks[15], (L, N_BRANCH, BRANCH_W, D_MODEL), BRANCH_W ** -0.5),
        "w_out": nrm(ks[16], (L, D_MODEL, D_MODEL), D_MODEL ** -0.5 * res_scale),
        "g_ffn": gain(ks[17], (L, D_MODEL)),
        "w_up": nrm(ks[18], (L, D_MODEL, 2 * D_FF), D_MODEL ** -0.5),
        "ffn_conv_w": nrm(ks[19], (L, FFN_CONV_K, 2 * D_FF), FFN_CONV_K ** -0.5),
        "ffn_conv_b": nrm(ks[20], (L, 2 * D_FF), 0.02),
        "w_down": nrm(ks[21], (L, D_FF, D_MODEL), D_FF ** -0.5 * res_scale),
    }

def reference(x, g_mix, w_in, lb_logits, g_hg_out, g_q_lat, w_uq, g_kv_lat, w_ukv,
              g_qk_q, g_qk_k, conv_w, conv_b, conv_ln_g, conv_ln_b, w_branch, w_out,
              g_ffn, w_up, ffn_conv_w, ffn_conv_b, w_down):
    b, s, _ = x.shape
    pos = jnp.arange(s)
    lb_all = jnp.cumsum(jax.nn.softmax(lb_logits.astype(F32), axis=0), axis=0)
    lb_all = lb_all - lb_all[0:1]
    offs = np.cumsum(np.array(IN_COLS))[:-1].tolist()
    for l in range(DEPTH):
        h = _rmsnorm(x, g_mix[l])
        proj = h @ w_in[l]
        (hq, hf, hv, hg, cq, ckv, kr, cu, sq, sk, sv, gl) = jnp.split(proj, offs, axis=-1)
        y_a = _hgrn2_branch(hq, hf, hv, hg, lb_all[l], g_hg_out[l])
        y_b = _mla_branch(cq, ckv, kr, g_q_lat[l], w_uq[l], g_kv_lat[l], w_ukv[l],
                          g_qk_q[l], g_qk_k[l], pos)
        y_c = _conformer_conv_branch(cu, conv_w[l], conv_b[l], conv_ln_g[l], conv_ln_b[l])
        y_d = _stick_breaking_branch(sq, sk, sv)
        ys = jnp.stack([y_a, y_b, y_c, y_d], axis=2)
        br = jnp.einsum('bsnc,ncd->bsnd', ys, w_branch[l])
        gates = jax.nn.sigmoid(gl.reshape(b, s, N_BRANCH, D_MODEL))
        merged = jnp.einsum('bsnd,bsnd->bsd', gates, br)
        x = x + merged @ w_out[l]
        h2 = _rmsnorm(x, g_ffn[l])
        u = _causal_dwconv(h2 @ w_up[l], ffn_conv_w[l], ffn_conv_b[l])
        val, gate = jnp.split(u, 2, axis=-1)
        x = x + (jax.nn.silu(gate) * val) @ w_down[l]
    return x


_drawn_inputs = setup_inputs


def setup_inputs(seed=0):
    import zlib

    import numpy as np

    out = dict(_drawn_inputs(seed))
    spreads = {}
    factors = {'lb_logits': 42.143,
     'g_q_lat': 7.816,
     'g_kv_lat': 4.979,
     'g_qk_q': 7.784,
     'g_qk_k': 7.972,
     'conv_b': 5.632,
     'conv_ln_b': 8.0,
     'ffn_conv_b': 5.069}
    for name, (base, spread) in spreads.items():
        noise = np.random.default_rng([zlib.crc32(name.encode()), seed]).standard_normal(out[name].shape)
        drawn = base * np.exp(spread * noise) if base else spread * noise
        out[name] = __import__('jax').numpy.asarray(drawn.astype(out[name].dtype))
    for name, factor in factors.items():
        out[name] = (out[name] * factor).astype(out[name].dtype)
    return out
```

```python
from contextlib import ExitStack

import numpy as np
import concourse.bass as bass
from concourse import mybir

F32 = mybir.dt.float32
F16 = mybir.dt.float16
ALU = mybir.AluOpType
ACT = mybir.ActivationFunctionType
AX = mybir.AxisListType

P = 128
L = 2
T = 256
D = 1024
KT = D // P
TT = T // P
NH = 4
HD = 64
NOPE, ROPE = 64, 32
QK = NOPE + ROPE
CK = 31
FF = 2816
J = FF // 256
BW = 16
NB = T // BW
EPS = 1e-6
RAW = 3
RING = 6
WS = 64.0
IWS = 1.0 / WS
SLAB = 2048
START = 1
AHEAD = 4

PROJ = [(0, 256), (256, 256), (512, 256), (768, 256), (1024, 256), (1280, 160),
        (1440, 256), (1696, 256), (1952, 256), (2208, 256), (2464, 256)]
S_HQ, S_HF, S_HV, S_HG, S_CQ, S_KV, S_CA, S_CG, S_SQ, S_SK, S_SV = range(11)
S_GATE = len(PROJ)
S_BR = S_GATE + 16
S_WO = S_BR + 4
S_FF = S_WO + 4
NSLAB = S_FF + 3 * J
GATE0 = 2720
BRANCH_ORDER = [3, 2, 1, 0]


def slab_v(j):
    return S_FF + 3 * j - 1 if not (isinstance(j, int) and j == 0) else S_FF


def slab_g(j):
    return slab_v(j) + 1


def slab_d(j):
    return S_FF + 3 * j + 4 if not (isinstance(j, int) and j == J - 1) else S_FF + 3 * J - 1


CONST = {}
MIXP = {}
FFP = {}


def columns(table, spec):
    at = 0
    for name, width in spec:
        table[name] = (at, at + width)
        at += width
    return at


NCONST = columns(CONST, [("ident", P), ("headones", P), ("blk8", 8), ("ends", T), ("headmask", 2),
                         ("neg", 384), ("ge", 384), ("lt", 384), ("cos", 32), ("sin", 32),
                         ("one", 1), ("minushalf", 1)])
NMIXP = columns(MIXP, [("g_mix", KT), ("g_hg", 1), ("g_latent", 3), ("g_qk", 2 * QK),
                       ("conv_w", 2 * CK), ("conv_b", 2), ("ln_g", 2), ("ln_b", 2)])
NWU = 2 * NH * QK + NH * 128
NFFP = columns(FFP, [("g_ffn", KT), ("w", 3 * 2 * J * 2), ("b", 2 * J * 2)])


class Steps:

    def __init__(self, book, sem, name, start=0):
        self.sem, self.order, self.start = sem, [], start
        self.known = book.get(name, [])
        book[name] = self.order

    def mark(self, step):
        self.order.append(step)
        return self.sem

    def total(self, l):
        return l * len(self.known) + self.start

    def at(self, l, step):
        if step not in self.known:
            return 1
        return l * len(self.known) + (self.known.index(step) + 1 + self.start)


def program(nc, book, x, slabs, lb_logits, consts, mixp, wup, ffp, out):
    ctx = ExitStack()
    with ctx:
        def sb(name, shape, dt=F32):
            return ctx.enter_context(nc.sbuf_tensor(name, [P] + shape, dt))

        def sem(name):
            return ctx.enter_context(nc.semaphore(name))

        def steps(name, start=0):
            return Steps(book, sem(name), name, start)

        wf = sb("wf", [RAW, SLAB])
        wh = sb("wh", [RING, SLAB], F16)
        wl = sb("wl", [RING, SLAB], F16)
        xr = sb("xr", [TT, D])
        xn = sb("xn", [TT, D])
        hh = sb("hh", [KT, T], F16)
        hl = sb("hl", [KT, T], F16)
        h32 = sb("h32", [2, 2 * T])
        gates = sb("gates", [4, KT, T])
        mgtmp = sb("mgtmp", [2, 2 * T])
        fx = sb("fx", [4112])

        def view(tensor2, at, *dims):
            n = int(np.prod(dims))
            v_ = tensor2[:, at:at + n]
            names = " ".join("abcd"[:len(dims)])
            sizes = {x_: d_ for x_, d_ in zip("abcd", dims)}
            return v_.rearrange(f"p ({names}) -> p {names}", **sizes) if len(dims) > 1 else v_

        g0, g1, g2, g3 = (gates[:, b_, :, :].rearrange("p k t -> p (k t)") for b_ in range(4))
        g23 = gates[:, 2:4, :, :].rearrange("p b k t -> p (b k t)")
        xflat = xn[:, :, :].rearrange("p t d -> p (t d)")
        mg = view(xflat, 0, KT, T)
        mh, ml = hh, hl
        yh = sb("yh", [4, 2, T], F16)
        yl = sb("yl", [4, 2, T], F16)
        cst = sb("cst", [NCONST])
        pm = sb("pm", [NMIXP])
        pf = sb("pf", [NFFP])
        gql = sb("gql", [3])
        ftap = sb("ftap", [12 * J])
        stat = sb("stat", [64])

        def c_(name):
            return cst[:, CONST[name][0]:CONST[name][1]]

        def m_(name, a=0, n=None):
            lo, hi = MIXP[name]
            return pm[:, lo + a:(hi if n is None else lo + a + n)]

        def f_(name, a=0, n=None):
            lo, hi = FFP[name]
            return pf[:, lo + a:(hi if n is None else lo + a + n)]

        ident, headones = c_("ident"), c_("headones")

        ss, ms, rs = stat[:, 0:2], stat[:, 2:4], stat[:, 4:6]
        lat_ms, lat_rs = stat[:, 6:10], stat[:, 10:14]
        ln_ag, ln_ms, ln_rs = stat[:, 14:18], stat[:, 18:20], stat[:, 20:22]
        mx, nmx, den, rden = stat[:, 22:30], stat[:, 30:38], stat[:, 38:46], stat[:, 46:54]
        bnst = sb("bnst", [2, 6])
        qk_ss, qk_ms, qk_rs = sb("qk_ss", [16]), sb("qk_ms", [16]), sb("qk_rs", [16])
        lbx = sb("lbx", [8, 4])
        lbt, omlbt = sb("lbt", [L * 2]), sb("omlbt", [L * 2])
        lb, omlb = sb("lb", [2]), sb("omlb", [2])

        q, f, k, v, gg, o, pre, wlag = (sb(n, [2, T]) for n in ("q", "f", "k", "v", "gg", "o", "pre", "wlag"))
        f_in, f_first, f_next = view(g0, 0, 2, T), view(g0, 512, 2, T), view(g0, 1024, 2, T)
        kd = view(g0, 1536, 2, T)
        qdm = sb("qdm", [2, 2, T])
        plag = h32[:, :, :]
        olag = mgtmp[:, :, :]
        kdm = view(fx[:, :], 0, 8, TT * 256)
        vt = view(g1, 0, TT, 256)
        st = view(g23, 0, NB, 256)
        osq = view(fx[:, :], 1536, 2 * T)
        cqs, cqg = view(g1, 0, 2, T), view(g1, 512, 2, T)
        kvs, kvg = view(g1, 1024, T), view(g1, 1280, T)
        kr = view(g1, 1536, TT, ROPE)
        wu = view(g2, 0, NWU)
        qk = sb("qk", [16 * QK])
        prT = view(qk[:, :], 0, NH, 384)
        qk = view(qk[:, :], 0, 16, QK)
        qksq = view(xflat, 0, 16, QK)
        rt = view(xflat, 0, 4, 16, 16)
        vm = sb("vm", [TT, NH, HD])
        qkT = view(g3, 0, 2, NH, T)
        sc = view(xflat, 0, NH, 384)
        pr = sc
        sqT, skT = view(g1, 512, 2, T), view(g1, 1024, 2, T)
        sv = sb("sv", [TT, 256])
        beta = view(g2, 0, NH, 384)
        omb = view(fx[:, :], 0, NH, 384)
        wT = omb
        incl = view(fx[:, :], 1536, NH * 384 + 1)
        ca, sg_c = view(g0, 0, 2, T), view(g0, 512, 2, T)
        cu = sb("cu", [2, T + CK - 1])
        cacc = sb("cacc", [2, T])
        cn = view(fx[:, :], 3592, TT, 256)
        cz, csig = view(fx[:, :], 2048, 2, T), view(fx[:, :], 2560, 2, T)
        y32 = [osq, view(xflat, 1536, 2 * T), view(fx[:, :], 2048, 2 * T), view(fx[:, :], 3080, 2 * T)]
        orx = view(wlag[:, :, :].rearrange("p c t -> p (c t)"), 0, TT, 256)
        o_ms, o_rs = sb("o_ms", [8]), sb("o_rs", [8])
        u_v, u_g = view(fx[:, :], 0, 2, 2, T), view(fx[:, :], 1024, 2, 2, T)
        gh = view(fx[:, 2048:2560].bitcast(F16), 0, 2, 2, T)
        gl = view(fx[:, 2560:3072].bitcast(F16), 0, 2, 2, T)

        bank = [ctx.enter_context(nc.psum_tensor(f"bank{i}", [P, 512], F32)) for i in range(8)]

        const_in, logits_in, mixp_in, wu_in, ffp_in = (sem(n) for n in ("const_in", "logits_in", "mixp_in", "wu_in", "ffp_in"))
        x_in = [sem(f"x_in{t}") for t in range(TT)]
        slab_in = [sem(f"slab_in{i}") for i in range(RAW)]
        high_ready = sem("high_ready")
        low_ready = sem("low_ready")
        slab_done = sem("slab_done")
        x_new = sem("x_new")
        setup = sem("setup")
        setup_act = sem("setup_act")
        pool_setup = sem("pool_setup")
        out_done = sem("out_done")
        nm_pe, nm_act, nm_dve, nm_pool = (steps(f"norm_{e}") for e in ("pe", "act", "dve", "pool"))
        hg_pe, hg_act, hg_dve, hg_pool = (steps(f"hgrn_{e}") for e in ("pe", "act", "dve", "pool"))
        la_pe, la_act, la_dve, la_pool = (steps(f"latent_{e}") for e in ("pe", "act", "dve", "pool"))
        cv_pe, cv_act, cv_dve, cv_pool = (steps(f"conv_{e}") for e in ("pe", "act", "dve", "pool"))
        sk_pe, sk_act, sk_dve, sk_pool = (steps(f"stick_{e}") for e in ("pe", "act", "dve", "pool"))
        mg_pe, mg_act, mg_pool = (steps(f"merge_{e}") for e in ("pe", "act", "pool"))
        mg_dve = steps("merge_dve", START)
        ff_act, ff_dve = sem("ffn_act"), sem("ffn_dve")
        ff_tap = sem("ffn_taps_scaled")

        FA = ["v0", "v1", "g0", "g1", "silu", "high"]
        FD = ["v0a", "v1a", "v0b", "v1b", "g0a", "g1a", "g0b", "g1b", "mul", "low"]

        def ffa(l, j, step):
            return l * (J * len(FA)) + j * len(FA) + (FA.index(step) + 1)

        def ffd(l, j, step):
            return l * (J * len(FD)) + j * len(FD) + (FD.index(step) + 1 + START)

        def x_at(l, n):
            return l * 8 + (n + 3)

        def slab_at(l, n):
            return l * NSLAB + (n + 1)

        def low_at(l, n):
            return l * NSLAB + (n + 1 + RAW)

        def done_at(l, n):
            return l * NSLAB + (n + 1 + RING)

        uses = {}
        last_use = {}
        ring_at = [0]

        def use(name, reader, label, banks=6, where=None):
            b = where if where is not None else ring_at[0] % banks
            if where is None:
                ring_at[0] += 1
            uses[name] = (b, last_use.get(b))
            last_use[b] = (reader, label)

        for kp in range(4):
            use(f"n1{kp}", nm_dve, f"1lo{kp}")
        proj_reader = {S_HQ: (hg_dve, "q"), S_HF: (hg_act, "smf"), S_HV: (hg_act, "v"), S_HG: (hg_dve, "gg"),
                       S_CQ: (la_act, "cqg1"), S_KV: (la_act, "kr"), S_CA: (cv_act, "ca"),
                       S_CG: (cv_act, "sg"), S_SQ: (sk_act, "sq"), S_SK: (sk_act, "sk"), S_SV: (sk_act, "sv")}
        pieces = {}

        def after(n, *names):
            pieces.setdefault(n, []).extend(names)

        for d in range(BW):
            after(4 + d, f"lag{d}")
        after(7, "lat_ss", "lat_q0", "lat_q1", "lat_kv0", "lat_kv1")
        after(8, "kdT", "vT")
        for r in range(8):
            after(10 + r // 2, f"ds{r}")
        after(14, "inter0", "inter1", "z0", "z1", "z2", "z3")
        after(15, "qkT0", "qkT1", "qkT2", "qkT3")
        after(16, "s0", "s1", "s2", "s3")
        after(18, "wT0", "wT1", "wT2", "wT3")
        after(19, "lnT")
        after(20, "skv")
        after(21, "pT0", "pT1", "pT2", "pT3", "oss")
        after(22, "lnB", "lav")
        after(23, "orT")
        small_reader = {"lat_ss": (la_dve, "lat_ms1"), "lat_q0": (la_act, "q0"), "lat_q1": (la_act, "q1"),
                        "lat_kv0": (la_act, "vm0"), "lat_kv1": (la_act, "vm1"), "kdT": (hg_act, "kdm7"), "vT": (hg_act, "vt"),
                        "inter0": (hg_dve, "oi01"), "inter1": (hg_dve, "oi11"), "lnT": (cv_dve, "cn1"), "lnB": (cv_act, "sig1"),
                        "skv": (sk_act, "y"), "lav": (la_act, "y"), "oss": (hg_dve, "o_ms"), "orT": (hg_dve, "on")}
        for d in range(BW):
            small_reader[f"lag{d}"] = (hg_dve, f"t{d}")
        for r in range(8):
            small_reader[f"ds{r}"] = (hg_dve, f"st{min(2 * r + 2, NB - 1)}1")
        for h in range(4):
            small_reader[f"z{h}"] = (sk_act, f"omb{h}")
            small_reader[f"qkT{h}"] = (la_act, f"qkT{h}")
            small_reader[f"s{h}"] = (la_dve, f"sc{h}")
            small_reader[f"wT{h}"] = (sk_act, f"wT{h}")
            small_reader[f"pT{h}"] = (la_act, f"pT{h}")
        for n in range(S_BR):
            use(f"slab{n}", *(proj_reader[n] if n < S_GATE else (mg_act, f"gate{n - S_GATE}")))
            for name in pieces.get(n, []):
                if name.startswith("lag"):
                    use(name, *small_reader[name], where=6 + int(name[3:]) % 2)
                else:
                    use(name, *small_reader[name])
        for i in range(4):
            for r in range(4):
                use(f"br{i}{r}", mg_dve, f"m{i}{r}")
        for a in range(4):
            uses[f"wo{a}"] = (4 + a, last_use.get(4 + a))
            last_use[4 + a] = None
        for kp in range(4):
            use(f"n2{kp}", nm_dve, f"2lo{kp}", where=kp)

        def bank_of(name):
            return bank[uses[name][0]]

        def wait_bank(eng, l, name):
            before = uses[name][1]
            if before is not None:
                eng.wait_ge(before[0].sem, before[0].at(l, before[1]))

        def blocks(ap2):
            return ap2.rearrange("p c (b w) -> p (c b) w", w=BW)

        def tap_of(j, half, c, tap):
            lo = (half * 2 + c) * 3 + tap
            return ftap[:, lo + j * 12:lo + j * 12 + 1] if isinstance(j, int) else ftap[:, bass.ds(j * 12 + lo, 1)]

        def bias_of(j, half, c):
            lo = FFP["b"][0] + half * 2 + c
            return pf[:, lo + j * 4:lo + j * 4 + 1] if isinstance(j, int) else pf[:, bass.ds(j * 4 + lo, 1)]

        block = ctx.enter_context(nc.Block())

        @block.sync
        def _(sp):
            sp.dma_start(lbx[:, 0, :], lb_logits).then_inc(logits_in, 16)
            for t in range(TT):
                sp.dma_start(xr[:, t, :], x[t * P:(t + 1) * P, :]).then_inc(x_in[t], 16)
            sp.dma_start(cst[:, :], consts).then_inc(const_in, 16)
            with sp.Fori(0, L) as l:
                sp.wait_ge(mg_dve.sem, mg_dve.total(l))
                sp.wait_ge(low_ready, low_at(l, last_in_slot(0, RAW) - NSLAB))
                sp.dma_start(pm[:, :], mixp[l, :, :]).then_inc(mixp_in, 16)

                def load(n, slot):
                    sp.dma_start(wf[:, slot, :], slabs[l, n, :, :]).then_inc(slab_in[slot], 16)

                load(0, 0)
                for n in range(1, S_FF + 5):
                    sp.wait_ge(low_ready, low_at(l, n - RAW if n >= RAW else last_in_slot(n, RAW) - NSLAB))
                    load(n, n % RAW)
                    if n == RAW:
                        sp.dma_start(wu, wup[l, :, :]).then_inc(wu_in, 16)
                    if n == 11:
                        sp.wait_ge(ff_dve, l * (J * len(FD)) + START)
                        sp.dma_start(pf[:, :], ffp[l, :, :]).then_inc(ffp_in, 16)
                with sp.Fori(0, 4) as i:
                    for m in range(6):
                        n = i * 6 + (S_FF + 5 + m)
                        sp.wait_ge(low_ready, low_at(l, i * 6 + (S_FF + 5 + m - RAW)))
                        load(n, (S_FF + 5 + m) % RAW)
                for n in range(S_FF + 29, NSLAB):
                    sp.wait_ge(low_ready, low_at(l, n - RAW))
                    load(n, n % RAW)
            for t in range(TT):
                sp.wait_ge(x_new, x_at(L, 2 * t - 2))
                sp.dma_start(out[t * P:(t + 1) * P, :], xr[:, t, :]).then_inc(out_done, 16)
            sp.wait_ge(out_done, 16 * TT)

        @block.tensor
        def _(pe):
            pe.sem_inc(slab_done, RING)
            pe.wait_ge(const_in, 16)
            pe.wait_ge(pool_setup, 1)

            def mm3(o_, wt_h, wt_l, a_h, a_l, first, last, stationary_weight):
                passes = ((wt_h, a_h), (wt_h, a_l), (wt_l, a_h))
                for i_, (w_, a_) in enumerate(passes):
                    lt, rh = (w_, a_) if stationary_weight else (a_, w_)
                    ins = nc.tensor.matmul(o_, lt, rh, start=first and i_ == 0, stop=last and i_ == 2)
                return ins

            def mm(o_, lt, rh, first=True, last=True):
                return nc.tensor.matmul(o_, lt, rh, start=first, stop=last)

            def tr(o_, in_, n=P):
                return nc.tensor.transpose(o_, in_, ident)

            def norm(l, w):
                for t in range(TT):
                    pe.wait_ge(nm_dve.sem, nm_dve.at(l, f"{w}xn{t}"))
                    for kp in range(4):
                        if t == 0:
                            wait_bank(pe, l, f"n{w}{kp}")
                        b = bank_of(f"n{w}{kp}")
                        for c in range(2):
                            ins = tr(b[:, c * T + t * P:c * T + t * P + P], xn[:, t, (2 * kp + c) * P:(2 * kp + c + 1) * P])
                        if t == TT - 1:
                            ins.then_inc(nm_pe.mark(f"{w}T{kp}"), 1)

            def column_slab(b, slot, chunks=2, after_norm=None):
                for c in range(chunks):
                    for kt in range(KT):
                        if after_norm is not None and c == 0 and kt % 2 == 0:
                            l_, w_ = after_norm
                            pe.wait_ge(nm_dve.sem, nm_dve.at(l_, f"{w_}lo{kt // 2}"))
                        a = kt * 256 + c * P
                        ins = mm3(b[:, c * T:(c + 1) * T], wh[:, slot, a:a + P], wl[:, slot, a:a + P],
                                  hh[:, kt, :], hl[:, kt, :], kt == 0, kt == KT - 1, True)
                return ins

            def token_columns(b, slot, off, width, at):
                for t in range(TT):
                    for kt in range(KT):
                        a = kt * 256 + off
                        ins = mm3(b[:, at + t * width:at + (t + 1) * width], wh[:, slot, a:a + width],
                                  wl[:, slot, a:a + width], hh[:, kt, t * P:(t + 1) * P],
                                  hl[:, kt, t * P:(t + 1) * P], kt == 0, kt == KT - 1, False)
                return ins

            def row_slab(slot, ah, al, first, last):
                for t in range(TT):
                    for n in range(2):
                        for kt in range(2):
                            a = kt * D + n * 512
                            ins = mm3(bank[4 + 2 * t + n][:, :], wh[:, slot, a:a + 512], wl[:, slot, a:a + 512],
                                      ah[:, kt, t * P:(t + 1) * P], al[:, kt, t * P:(t + 1) * P],
                                      first and kt == 0, last and kt == 1, False)
                return ins

            with pe.Fori(0, L) as l:
                norm(l, 1)

                def piece(name):
                    b = bank_of(name)
                    wait_bank(pe, l, name)
                    if name.startswith("lag"):
                        d = int(name[3:])
                        n = 2 * NB * (BW - d)
                        pe.wait_ge(hg_pool.sem, hg_pool.at(l, f"p{d}"))
                        mm(b[:, 0:n], headones, plag[:, d % 2, 0:n]).then_inc(hg_pe.mark(name), 1)
                    elif name == "lat_ss":
                        pe.wait_ge(la_act.sem, la_act.at(l, "kr"))
                        for t in range(TT):
                            for c in range(2):
                                mm(b[:, t:t + 1], cqs[:, c, t * P:(t + 1) * P], c_("one"), c == 0, c == 1)
                        for t in range(TT):
                            ins = mm(b[:, 2 + t:3 + t], kvs[:, t * P:(t + 1) * P], c_("one"))
                        ins.then_inc(la_pe.mark(name), 1)
                    elif name.startswith("lat_q"):
                        t = int(name[-1])
                        pe.wait_ge(wu_in, l * 16 + 16)
                        for c in range(2):
                            ins = mm(b[:, 0:NH * QK], cqg[:, c, t * P:(t + 1) * P], wu[:, c * NH * QK:(c + 1) * NH * QK], c == 0, c == 1)
                        ins.then_inc(la_pe.mark(name), 1)
                    elif name.startswith("lat_kv"):
                        t = int(name[-1])
                        mm(b[:, :], kvg[:, t * P:(t + 1) * P], wu[:, 2 * NH * QK:NWU]).then_inc(la_pe.mark(name), 1)
                    elif name == "kdT":
                        pe.wait_ge(hg_pool.sem, hg_pool.at(l, "kd"))
                        for t in range(TT):
                            for c in range(2):
                                ins = tr(b[:, t * 256 + c * P:t * 256 + (c + 1) * P], kd[:, c, t * P:(t + 1) * P])
                        ins.then_inc(hg_pe.mark(name), 1)
                    elif name == "vT":
                        for t in range(TT):
                            for c in range(2):
                                ins = tr(b[:, t * 256 + c * P:t * 256 + (c + 1) * P], v[:, c, t * P:(t + 1) * P])
                        ins.then_inc(hg_pe.mark(name), 1)
                    elif name.startswith("ds"):
                        r = int(name[2:])
                        if r == 0:
                            pe.wait_ge(hg_act.sem, hg_act.at(l, "vt"))
                        for e in range(2):
                            bl = 2 * r + e
                            if bl == NB - 1:
                                continue
                            t = bl // 8
                            for c in range(2):
                                ins = mm(b[:, e * 256 + c * P:e * 256 + (c + 1) * P],
                                         kdm[:, bl % 8, t * 256 + c * P:t * 256 + (c + 1) * P],
                                         vt[:, t, c * P:(c + 1) * P])
                        ins.then_inc(hg_pe.mark(name), 1)
                    elif name.startswith("inter"):
                        pe.wait_ge(hg_dve.sem, hg_dve.at(l, f"st{NB - 1}1"))
                        r = int(name[5])
                        for bl in range(max(1, 8 * r), 8 * r + 8):
                            for c in range(2):
                                a = c * 256 + (bl % 8) * 2 * BW
                                ins = mm(b[:, a:a + 2 * BW], st[:, bl, c * P:(c + 1) * P], qdm[:, :, c, bl * BW:(bl + 1) * BW])
                        ins.then_inc(hg_pe.mark(name), 1)
                    elif name == "oss":
                        pe.wait_ge(hg_act.sem, hg_act.at(l, "osq"))
                        for t in range(TT):
                            for c in range(2):
                                ins = mm(b[:, t * 4 + c * 2:t * 4 + c * 2 + 2], osq[:, c * T + t * P:c * T + (t + 1) * P], c_("headmask"))
                        ins.then_inc(hg_pe.mark(name), 1)
                    elif name == "orT":
                        pe.wait_ge(hg_dve.sem, hg_dve.at(l, "orx"))
                        for c in range(2):
                            for t in range(TT):
                                ins = tr(b[:, c * T + t * P:c * T + (t + 1) * P], orx[:, t, c * P:(c + 1) * P])
                        ins.then_inc(hg_pe.mark(name), 1)
                    elif name[0] == "z":
                        h = int(name[1])
                        r0 = (h % 2) * HD
                        if h == 0:
                            pe.wait_ge(sk_act.sem, sk_act.at(l, "sv"))
                        mm(b[:, 0:P], sqT[r0:r0 + HD, h // 2, 0:P], skT[r0:r0 + HD, h // 2, 0:P])
                        mm(b[:, P:P + T], sqT[r0:r0 + HD, h // 2, P:T], skT[r0:r0 + HD, h // 2, :]).then_inc(sk_pe.mark(name), 1)
                    elif name.startswith("qkT"):
                        u = int(name[3])
                        if u == 0:
                            pe.wait_ge(la_pool.sem, la_pool.at(l, "rot3"))
                        for e in range(2):
                            for t in range(TT):
                                n = (u // 2) * 8 + t * 4 + (u % 2) * 2 + e
                                ins = nc.tensor.transpose(b[0:QK, e * T + t * P:e * T + (t + 1) * P], qk[:, n, :], ident)
                        ins.then_inc(la_pe.mark(name), 1)
                    elif name[0] == "s" and name[1].isdigit():
                        h = int(name[1])
                        if h == 0:
                            pe.wait_ge(la_act.sem, la_act.at(l, "qkT3"))
                        mm(b[:, 0:P], qkT[0:QK, 0, h, 0:P], qkT[0:QK, 1, h, 0:P])
                        mm(b[:, P:P + T], qkT[0:QK, 0, h, P:T], qkT[0:QK, 1, h, :]).then_inc(la_pe.mark(name), 1)
                    elif name.startswith("wT") or name.startswith("pT"):
                        h = int(name[2])
                        src = beta if name[0] == "w" else pr
                        if h == 0:
                            s_, lab = (sk_pool, "w2") if name[0] == "w" else (la_pool, "pn1")
                            pe.wait_ge(s_.sem, s_.at(l, lab))
                        for e in range(3):
                            ins = tr(b[:, e * P:(e + 1) * P], src[:, h, e * P:(e + 1) * P])
                        ins.then_inc((sk_pe if name[0] == "w" else la_pe).mark(name), 1)
                    elif name in ("skv", "lav"):
                        s_, pe_s, src = (sk_act, sk_pe, wT) if name == "skv" else (la_act, la_pe, prT)
                        pe.wait_ge(s_.sem, s_.at(l, "wT3" if name == "skv" else "pT3"))
                        for h in range(NH):
                            r0 = (h % 2) * HD
                            o_ = b[r0:r0 + HD, (h // 2) * T:(h // 2 + 1) * T]
                            vv = [sv[:, t, h * HD:(h + 1) * HD] if name == "skv" else vm[:, t, h, :] for t in range(TT)]
                            mm(o_[:, 0:P], vv[0], src[:, h, 0:P])
                            mm(o_[:, P:T], vv[0], src[:, h, P:2 * P], True, False)
                            ins = mm(o_[:, P:T], vv[1], src[:, h, 2 * P:3 * P], False, True)
                        ins.then_inc(pe_s.mark(name), 1)
                    elif name == "lnT":
                        pe.wait_ge(cv_dve.sem, cv_dve.at(l, f"tap{CK - 1}1"))
                        for t in range(TT):
                            for c in range(2):
                                ins = tr(b[:, t * 256 + c * P:t * 256 + (c + 1) * P], cacc[:, c, t * P:(t + 1) * P])
                        ins.then_inc(cv_pe.mark(name), 1)
                    elif name == "lnB":
                        pe.wait_ge(cv_dve.sem, cv_dve.at(l, "cn1"))
                        for c in range(2):
                            for t in range(TT):
                                ins = tr(b[:, c * T + t * P:c * T + (t + 1) * P], cn[:, t, c * P:(c + 1) * P])
                        ins.then_inc(cv_pe.mark(name), 1)
                    else:
                        raise ValueError(name)

                for n in range(S_BR):
                    pe.wait_ge(low_ready, low_at(l, n))
                    wait_bank(pe, l, f"slab{n}")
                    b, slot = bank_of(f"slab{n}"), n % RING
                    if n == S_KV:
                        column_slab(b, slot, 1)
                        ins = token_columns(b, slot, P, ROPE, T)
                    elif n == S_SV:
                        ins = token_columns(b, slot, 0, 256, 0)
                    else:
                        ins = column_slab(b, slot, after_norm=(l, 1) if n == 0 else None)
                    ins.then_inc(slab_done, 1)
                    for name in pieces.get(n, []):
                        piece(name)
                ready = {3: (sk_dve, "lo"), 2: (cv_dve, "lo"), 1: (la_dve, "lo"), 0: (hg_dve, "lo")}
                for i, br in enumerate(BRANCH_ORDER):
                    n = S_BR + i
                    slot = n % RING
                    pe.wait_ge(low_ready, low_at(l, n))
                    pe.wait_ge(ready[br][0].sem, ready[br][0].at(l, ready[br][1]))
                    for r in range(4):
                        wait_bank(pe, l, f"br{i}{r}")
                        b = bank_of(f"br{i}{r}")
                        for c in range(2):
                            for kt in range(2):
                                a = kt * D + (2 * r + c) * P
                                ins = mm3(b[:, c * T:(c + 1) * T], wh[:, slot, a:a + P], wl[:, slot, a:a + P],
                                          yh[:, br, kt, :], yl[:, br, kt, :], kt == 0, kt == 1, True)
                        if r < 3:
                            ins.then_inc(mg_pe.mark(f"br{i}{r}"), 1)
                        else:
                            ins.then_inc(slab_done, 1)
                for a in range(4):
                    wait_bank(pe, l, f"wo{a}")
                for s_ in range(4):
                    n = S_WO + s_
                    pe.wait_ge(low_ready, low_at(l, n))
                    pe.wait_ge(mg_dve.sem, mg_dve.at(l, f"lo{s_}"))
                    row_slab(n % RING, mh[:, 2 * s_:2 * s_ + 2, :], ml[:, 2 * s_:2 * s_ + 2, :],
                             s_ == 0, s_ == 3).then_inc(slab_done, 1)
                norm(l, 2)

                def up_step(j, jp, slot_v, slot_g):
                    for half, n, slot in ((0, slab_v(j), slot_v), (1, slab_g(j), slot_g)):
                        pe.wait_ge(low_ready, low_at(l, n))
                        if not isinstance(j, int) or j >= 2:
                            pe.wait_ge(ff_dve, ffd(l, j - 2, "v1b" if half == 0 else "g1b"))
                        column_slab(bank[2 * jp + half], slot,
                                    after_norm=(l, 2) if isinstance(j, int) and j == 0 and half == 0 else None).then_inc(slab_done, 1)

                def down_step(j, jp, slot, first, last):
                    pe.wait_ge(low_ready, low_at(l, slab_d(j)))
                    pe.wait_ge(ff_dve, ffd(l, j, "low"))
                    row_slab(slot, gh[:, jp], gl[:, jp], first, last).then_inc(slab_done, 1)

                up_step(0, 0, slab_v(0) % RING, slab_g(0) % RING)
                up_step(1, 1, slab_v(1) % RING, slab_g(1) % RING)
                pe.wait_ge(x_new, x_at(l, 4))
                down_step(0, 0, slab_d(0) % RING, True, False)
                with pe.Fori(0, (J - 3) // 2) as i:
                    up_step(i * 2 + 2, 0, slab_v(2) % RING, slab_g(2) % RING)
                    down_step(i * 2 + 1, 1, slab_d(1) % RING, False, False)
                    up_step(i * 2 + 3, 1, slab_v(3) % RING, slab_g(3) % RING)
                    down_step(i * 2 + 2, 0, slab_d(2) % RING, False, False)
                up_step(J - 1, 0, slab_v(J - 1) % RING, slab_g(J - 1) % RING)
                down_step(J - 2, 1, slab_d(J - 2) % RING, False, False)
                down_step(J - 1, 0, slab_d(J - 1) % RING, False, True)

        @block.scalar
        def _(act):
            def high(l, n, slot, raw, uses_before, done):
                act.wait_ge(slab_in[raw], l * (16 * PER_SLOT[raw]) + (uses_before + 1) * 16)
                act.wait_ge(slab_done, done)
                nc.scalar.activation(wh[:, slot, :], wf[:, raw, :], ACT.Copy, scale=WS).then_inc(high_ready, 1)

            def high_of(l, n):
                high(l, n, n % RING, n % RAW, n // RAW,
                     done_at(l, n - RING if n >= RING else last_in_slot(n, RING) - NSLAB))

            act.wait_ge(setup, 3)
            nc.scalar.activation(lbx[:, 3, :], lbx[:, 2, :], ACT.Exp).then_inc(setup_act, 1)
            
            def norm(l, w, extra):
                for t in range(TT):
                    act.wait_ge(x_new, x_at(l, (0 if w == 1 else 4) + 2 * t - 2))
                    nc.scalar.activation(xn[:, t, :], xr[:, t, :], ACT.Square, accum_out=ss[:, t:t + 1]).then_inc(nm_act.mark(f"{w}sq{t}"), 1)
                for n in extra:
                    high_of(l, n)
                for kp in range(4):
                    act.wait_ge(nm_pe.sem, nm_pe.at(l, f"{w}T{kp}"))
                    for c in range(2):
                        g = m_("g_mix", 2 * kp + c, 1) if w == 1 else f_("g_ffn", 2 * kp + c, 1)
                        nc.scalar.activation(hh[:, 2 * kp + c, :], bank_of(f"n{w}{kp}")[:, c * T:(c + 1) * T],
                                             ACT.Copy, scale=g).then_inc(nm_act.mark(f"{w}hi{kp}{c}"), 1)

            with act.Fori(0, L) as l:
                act.wait_ge(mixp_in, l * 16 + 16)
                norm(l, 1, [0])
                for n in range(1, AHEAD):
                    high_of(l, n)

                def task(name):
                    b = bank_of(name) if name in uses else None
                    if name == "kdT":
                        act.wait_ge(hg_pe.sem, hg_pe.at(l, name))
                        for e in range(8):
                            nc.scalar.activation(kdm[:, e, :], b[:, :], ACT.Copy, scale=cst[:, CONST["blk8"][0] + e:CONST["blk8"][0] + e + 1]).then_inc(hg_act.mark(f"kdm{e}"), 1)
                    elif name == "vT":
                        act.wait_ge(hg_pe.sem, hg_pe.at(l, name))
                        nc.scalar.activation(vt[:, :, :].rearrange("p t c -> p (t c)"), b[:, :], ACT.Copy).then_inc(hg_act.mark("vt"), 1)
                    elif name.startswith("lat_q"):
                        t = int(name[-1])
                        act.wait_ge(la_pe.sem, la_pe.at(l, name))
                        act.wait_ge(la_pool.sem, la_pool.at(l, "lat_rs"))
                        nc.scalar.activation(qk[:, 4 * t:4 * t + 4, :].rearrange("p h c -> p (h c)"), b[:, 0:NH * QK], ACT.Copy,
                                             scale=lat_rs[:, t:t + 1]).then_inc(la_act.mark(f"q{t}"), 1)
                    elif name.startswith("lat_kv"):
                        t = int(name[-1])
                        act.wait_ge(la_pe.sem, la_pe.at(l, name))
                        bv = b[:, :].rearrange("p (h c) -> p h c", h=NH)
                        nc.scalar.activation(qk[:, 8 + 4 * t:12 + 4 * t, 0:NOPE], bv[:, :, 0:NOPE], ACT.Copy,
                                             scale=lat_rs[:, 2 + t:3 + t]).then_inc(la_act.mark(f"k{t}"), 1)
                        nc.scalar.activation(vm[:, t, :, :], bv[:, :, NOPE:P], ACT.Copy,
                                             scale=lat_rs[:, 2 + t:3 + t]).then_inc(la_act.mark(f"vm{t}"), 1)
                    elif name[0] == "z":
                        h = int(name[1])
                        act.wait_ge(sk_pe.sem, sk_pe.at(l, name))
                        nc.scalar.activation(beta[:, h, :], b[:, 0:384], ACT.Sigmoid).then_inc(sk_act.mark(f"beta{h}"), 1)
                        nc.scalar.activation(omb[:, h, :], b[:, 0:384], ACT.Sigmoid, scale=-1.0).then_inc(sk_act.mark(f"omb{h}"), 1)
                    elif name.startswith("qkT"):
                        u = int(name[3])
                        act.wait_ge(la_pe.sem, la_pe.at(l, name))
                        nc.scalar.activation(qkT[0:QK, u // 2, 2 * (u % 2):2 * (u % 2) + 2, :].rearrange("p h t -> p (h t)"), b[0:QK, :], ACT.Copy).then_inc(la_act.mark(name), 1)
                    elif name == "exps":
                        act.wait_ge(la_dve.sem, la_dve.at(l, "nmx"))
                        for h in range(NH):
                            for t in range(TT):
                                a, w_ = (0, P) if t == 0 else (P, T)
                                nc.scalar.activation(pr[:, h, a:a + w_], sc[:, h, a:a + w_], ACT.Exp, bias=nmx[:, t * 4 + h:t * 4 + h + 1],
                                                     scale=QK ** -0.5, accum_out=den[:, t * 4 + h:t * 4 + h + 1]).then_inc(la_act.mark(f"exp{h}{t}"), 1)
                    elif name.startswith("wT") or name.startswith("pT"):
                        h = int(name[2])
                        s_, a_s, dst = (sk_pe, sk_act, wT) if name[0] == "w" else (la_pe, la_act, prT)
                        act.wait_ge(s_.sem, s_.at(l, name))
                        nc.scalar.activation(dst[:, h, :], b[:, 0:384], ACT.Copy).then_inc(a_s.mark(name), 1)
                    elif name in ("skv", "lav"):
                        s_, a_s, i_ = (sk_pe, sk_act, 3) if name == "skv" else (la_pe, la_act, 1)
                        act.wait_ge(s_.sem, s_.at(l, name))
                        nc.scalar.activation(y32[i_], b[:, :], ACT.Copy).then_inc(a_s.mark("y"), 1)
                        act.wait_ge(a_s.sem, a_s.at(l, "y"))
                        nc.scalar.activation(yh[:, i_, :, :].rearrange("p c t -> p (c t)"), y32[i_], ACT.Copy).then_inc(a_s.mark("hi"), 1)
                    elif name == "osq":
                        act.wait_ge(hg_dve.sem, hg_dve.at(l, f"o{BW - 1}"))
                        nc.scalar.activation(osq, o[:, :, :].rearrange("p c t -> p (c t)"), ACT.Square).then_inc(hg_act.mark("osq"), 1)
                    elif name == "hgy":
                        act.wait_ge(hg_dve.sem, hg_dve.at(l, "y"))
                        nc.scalar.activation(yh[:, 0, :, :].rearrange("p c t -> p (c t)"), y32[0], ACT.Copy).then_inc(hg_act.mark("hi"), 1)
                    elif name == "lnB":
                        act.wait_ge(cv_pe.sem, cv_pe.at(l, name))
                        for c in range(2):
                            nc.scalar.activation(cz[:, c, :], b[:, c * T:(c + 1) * T], ACT.Identity, scale=m_("ln_g", c, 1), bias=m_("ln_b", c, 1)).then_inc(cv_act.mark(f"z{c}"), 1)
                        for c in range(2):
                            nc.scalar.activation(csig[:, c, :], b[:, c * T:(c + 1) * T], ACT.Sigmoid, scale=m_("ln_g", c, 1), bias=m_("ln_b", c, 1)).then_inc(cv_act.mark(f"sig{c}"), 1)
                    elif name == "cvy":
                        act.wait_ge(cv_pool.sem, cv_pool.at(l, "y"))
                        nc.scalar.activation(yh[:, 2, :, :].rearrange("p c t -> p (c t)"), y32[2], ACT.Copy).then_inc(cv_act.mark("hi"), 1)
                    else:
                        raise ValueError(name)

                tasks = {7: ["lat_q0", "lat_q1", "lat_kv0", "lat_kv1"], 8: ["kdT", "vT"],
                         14: ["z0", "z1", "z2", "z3"], 15: ["qkT0", "qkT1", "qkT2", "qkT3"],
                         17: ["exps"], 18: ["wT0", "wT1", "wT2", "wT3"], 20: ["skv", "osq"],
                         21: ["pT0", "pT1", "pT2", "pT3"], 22: ["lnB", "lav"], 24: ["cvy"], 25: ["hgy"]}

                def whole(ap2):
                    return ap2[:, :, :].rearrange("p c t -> p (c t)")

                for n in range(S_BR):
                    high_of(l, n + AHEAD)
                    b = bank_of(f"slab{n}")
                    act.wait_ge(slab_done, done_at(l, n))
                    if n == S_HQ:
                        nc.scalar.activation(whole(q), b[:, :], ACT.Sigmoid, scale=IWS).then_inc(hg_act.mark("sig_q"), 1)
                    elif n == S_HF:
                        nc.scalar.activation(whole(f), b[:, :], ACT.Sigmoid, scale=IWS).then_inc(hg_act.mark("sf"), 1)
                        nc.scalar.activation(whole(k), b[:, :], ACT.Sigmoid, scale=-IWS).then_inc(hg_act.mark("smf"), 1)
                    elif n == S_HV:
                        nc.scalar.activation(whole(v), b[:, :], ACT.Copy, scale=IWS).then_inc(hg_act.mark("v"), 1)
                    elif n == S_HG:
                        nc.scalar.activation(whole(gg), b[:, :], ACT.Sigmoid, scale=IWS).then_inc(hg_act.mark("sig_g"), 1)
                    elif n == S_CQ:
                        nc.scalar.activation(whole(cqs), b[:, :], ACT.Square, scale=IWS).then_inc(la_act.mark("cqs"), 1)
                        act.wait_ge(la_dve.sem, la_dve.at(l, "gql"))
                        for c in range(2):
                            nc.scalar.activation(cqg[:, c, :], b[:, c * T:(c + 1) * T], ACT.Copy, scale=gql[:, c:c + 1]).then_inc(la_act.mark(f"cqg{c}"), 1)
                    elif n == S_KV:
                        nc.scalar.activation(kvs, b[:, 0:T], ACT.Square, scale=IWS).then_inc(la_act.mark("kvs"), 1)
                        nc.scalar.activation(kvg, b[:, 0:T], ACT.Copy, scale=gql[:, 2:3]).then_inc(la_act.mark("kvg"), 1)
                        nc.scalar.activation(whole(kr), b[:, T:T + TT * ROPE], ACT.Copy, scale=IWS).then_inc(la_act.mark("kr"), 1)
                    elif n == S_CA:
                        nc.scalar.activation(whole(ca), b[:, :], ACT.Copy, scale=IWS).then_inc(cv_act.mark("ca"), 1)
                    elif n == S_CG:
                        nc.scalar.activation(whole(sg_c), b[:, :], ACT.Sigmoid, scale=IWS).then_inc(cv_act.mark("sg"), 1)
                    elif n == S_SQ:
                        nc.scalar.activation(whole(sqT), b[:, :], ACT.Copy, scale=HD ** -0.5 * IWS).then_inc(sk_act.mark("sq"), 1)
                    elif n == S_SK:
                        nc.scalar.activation(whole(skT), b[:, :], ACT.Copy, scale=IWS).then_inc(sk_act.mark("sk"), 1)
                    elif n == S_SV:
                        nc.scalar.activation(whole(sv), b[:, :], ACT.Copy, scale=IWS).then_inc(sk_act.mark("sv"), 1)
                    else:
                        g = n - S_GATE
                        nc.scalar.activation(gates[:, g // 4, 2 * (g % 4):2 * (g % 4) + 2, :].rearrange("p c t -> p (c t)"), b[:, :],
                                             ACT.Sigmoid, scale=IWS).then_inc(mg_act.mark(f"gate{g}"), 1)
                    for name in tasks.get(n, []):
                        task(name)
                for n in range(S_BR + AHEAD, S_FF):
                    high_of(l, n)
                for r in range(4):
                    act.wait_ge(mg_dve.sem, mg_dve.at(l, f"a3{r}"))
                    nc.scalar.activation(mh[:, 2 * r:2 * r + 2, :].rearrange("p c t -> p (c t)"),
                                         mg[:, 2 * r:2 * r + 2, :].rearrange("p c t -> p (c t)"), ACT.Copy).then_inc(mg_act.mark(f"hi{r}"), 1)
                for n in range(S_FF, S_FF + 5):
                    high_of(l, n)
                act.wait_ge(ffp_in, l * 16 + 16)
                norm(l, 2, [])

                def ff_step(j, jp):
                    for half, (u, n) in enumerate(((u_v, slab_v(j)), (u_g, slab_g(j)))):
                        act.wait_ge(slab_done, done_at(l, n))
                        if half == 0 and (not isinstance(j, int) or j >= 2):
                            act.wait_ge(ff_dve, ffd(l, j - 2, "low"))
                        for c in range(2):
                            tap, bias = tap_of(j, half, c, 2), bias_of(j, half, c)
                            nc.scalar.activation(u[:, jp, c, :], bank[2 * jp + half][:, c * T:(c + 1) * T], ACT.Identity,
                                                 scale=tap, bias=bias).then_inc(ff_act, 1)
                    act.wait_ge(ff_dve, ffd(l, j, "g1b"))
                    nc.scalar.activation(u_g[:, jp, :, :].rearrange("p c t -> p (c t)"), u_g[:, jp, :, :].rearrange("p c t -> p (c t)"), ACT.Silu).then_inc(ff_act, 1)
                    act.wait_ge(ff_dve, ffd(l, j, "mul"))
                    if not isinstance(j, int) or j >= 2:
                        act.wait_ge(slab_done, done_at(l, slab_d(j - 2)))
                    nc.scalar.activation(gh[:, jp, :, :].rearrange("p c t -> p (c t)"), u_v[:, jp, :, :].rearrange("p c t -> p (c t)"), ACT.Copy).then_inc(ff_act, 1)

                act.wait_ge(ff_tap, l + 1)
                ff_step(0, 0)
                for n in range(S_FF + 5, S_FF + 8):
                    high_of(l, n)
                ff_step(1, 1)
                with act.Fori(0, (J - 3) // 2) as i:
                    for e in range(2):
                        for m in range(3):
                            n0 = S_FF + 8 + 3 * e + m
                            high(l, None, n0 % RING, n0 % RAW, i * 2 + n0 // RAW, done_at(l, i * 6 + (n0 - RING)))
                        ff_step(i * 2 + (2 + e), e)
                high_of(l, NSLAB - 1)
                ff_step(J - 1, 0)

        @block.vector
        def _(dve):
            dve.sem_inc(mg_dve.sem, START)
            dve.sem_inc(ff_dve, START)
            dve.sem_inc(low_ready, RAW)
            dve.wait_ge(logits_in, 16)
            l0, l1 = lbx[:, 0, 0:2], lbx[:, 0, 2:4]
            nc.vector.tensor_tensor(lbx[:, 1, 0:2], l0, l1, ALU.max).then_inc(setup, 1)
            dve.wait_ge(setup, 1)
            nc.vector.tensor_tensor(lbx[:, 2, 0:2], l0, lbx[:, 1, 0:2], ALU.subtract).then_inc(setup, 1)
            nc.vector.tensor_tensor(lbx[:, 2, 2:4], l1, lbx[:, 1, 0:2], ALU.subtract).then_inc(setup, 1)
            dve.wait_ge(setup_act, 1)
            e0, e1 = lbx[:, 3, 0:2], lbx[:, 3, 2:4]
            nc.vector.tensor_tensor(lbx[:, 4, 0:2], e0, e1, ALU.add).then_inc(setup, 1)
            dve.wait_ge(setup, 4)
            nc.vector.reciprocal(lbx[:, 5, 0:2], lbx[:, 4, 0:2]).then_inc(setup, 1)
            dve.wait_ge(setup, 5)
            nc.vector.tensor_tensor(lbx[:, 6, 0:2], e0, lbx[:, 5, 0:2], ALU.mult).then_inc(setup, 1)
            nc.vector.tensor_tensor(lbx[:, 6, 2:4], e1, lbx[:, 5, 0:2], ALU.mult).then_inc(setup, 1)
            dve.wait_ge(setup, 7)
            nc.vector.tensor_tensor(lbx[:, 7, 0:2], lbx[:, 6, 0:2], lbx[:, 6, 2:4], ALU.add).then_inc(setup, 1)
            nc.vector.tensor_tensor(lbt[:, 0:2], lbx[:, 6, 0:2], lbx[:, 6, 0:2], ALU.subtract).then_inc(setup, 1)
            dve.wait_ge(setup, 9)
            nc.vector.tensor_tensor(lbt[:, 2:4], lbx[:, 7, 0:2], lbx[:, 6, 0:2], ALU.subtract).then_inc(setup, 1)
            dve.wait_ge(setup, 10)
            nc.vector.tensor_scalar(omlbt[:, :], lbt[:, :], -1.0, 1.0, ALU.mult, ALU.add).then_inc(setup, 1)
            dve.wait_ge(setup, 11)
            dve.wait_ge(x_in[0], 16)
            dve.sem_inc(x_new, 1)
            dve.wait_ge(x_in[1], 16)
            dve.sem_inc(x_new, 2)
            dve.wait_ge(const_in, 16)
            dve.wait_ge(pool_setup, 1)

            def TTo(out_, a, b, op):
                return nc.vector.tensor_tensor(out_, a, b, op)

            def STT(out_, a, s_, b, op0=ALU.mult, op1=ALU.add):
                return nc.vector.scalar_tensor_tensor(out=out_, in0=a, scalar=s_, in1=b, op0=op0, op1=op1)

            def own(s_, l, step):
                dve.wait_ge(s_.sem, s_.at(l, step))

            def whole(ap2):
                return ap2[:, :, :].rearrange("p c t -> p (c t)")

            with dve.Fori(0, L) as l:
                def split_at(n, slot, raw):
                    dve.wait_ge(high_ready, slab_at(l, n))
                    STT(wl[:, slot, :], wf[:, raw, :], WS, wh[:, slot, :], ALU.mult, ALU.subtract).then_inc(low_ready, 1)

                def split(n):
                    split_at(n, n % RING, n % RAW)

                def norm(l, w, extra):
                    for t in range(TT):
                        dve.wait_ge(nm_act.sem, nm_act.at(l, f"{w}sq{t}"))
                        nc.vector.tensor_scalar(ms[:, t:t + 1], ss[:, t:t + 1], 1.0 / D, EPS, ALU.mult, ALU.add).then_inc(nm_dve.mark(f"{w}ms{t}"), 1)
                    for t in range(TT):
                        dve.wait_ge(nm_pool.sem, nm_pool.at(l, f"{w}rs{t}"))
                        nc.vector.tensor_scalar(xn[:, t, :], xr[:, t, :], rs[:, t:t + 1], None, ALU.mult).then_inc(nm_dve.mark(f"{w}xn{t}"), 1)
                    for n in extra:
                        split(n)
                    for kp in range(4):
                        dve.wait_ge(nm_act.sem, nm_act.at(l, f"{w}hi{kp}1"))
                        for c in range(2):
                            g = m_("g_mix", 2 * kp + c, 1) if w == 1 else f_("g_ffn", 2 * kp + c, 1)
                            ins = STT(hl[:, 2 * kp + c, :], bank_of(f"n{w}{kp}")[:, c * T:(c + 1) * T], g,
                                      hh[:, 2 * kp + c, :], ALU.mult, ALU.subtract)
                        ins.then_inc(nm_dve.mark(f"{w}lo{kp}"), 1)

                def low_of(y, s_, act_s, i_):
                    dve.wait_ge(act_s.sem, act_s.at(l, "hi"))
                    nc.vector.tensor_tensor(yl[:, i_, :, :].rearrange("p c t -> p (c t)"), y32[i_],
                                            yh[:, i_, :, :].rearrange("p c t -> p (c t)"), ALU.subtract).then_inc(s_.mark("lo"), 1)

                def task(name):
                    b = bank_of(name) if name in uses else None
                    if name == "q":
                        dve.wait_ge(hg_act.sem, hg_act.at(l, "sig_q"))
                        STT(whole(q), bank_of("slab0")[:, :], IWS, whole(q), ALU.mult, ALU.mult).then_inc(hg_dve.mark("q"), 1)
                    elif name == "f":
                        nc.vector.tensor_copy(lb[:, :], lbt[:, bass.ds(l * 2, 2)]).then_inc(hg_dve.mark("lb"), 1)
                        nc.vector.tensor_copy(omlb[:, :], omlbt[:, bass.ds(l * 2, 2)]).then_inc(hg_dve.mark("omlb"), 1)
                        dve.wait_ge(hg_act.sem, hg_act.at(l, "smf"))
                        own(hg_dve, l, "omlb")
                        for c in range(2):
                            nc.vector.tensor_scalar(f[:, c, :], f[:, c, :], omlb[:, c:c + 1], lb[:, c:c + 1],
                                                    ALU.mult, ALU.add).then_inc(hg_dve.mark(f"f{c}"), 1)
                        for c in range(2):
                            nc.vector.tensor_scalar(k[:, c, :], k[:, c, :], omlb[:, c:c + 1], None,
                                                    ALU.mult).then_inc(hg_dve.mark(f"k{c}"), 1)
                        own(hg_dve, l, "f1")
                        dve.wait_ge(hg_pool.sem, hg_pool.at(l, "zero"))
                        fb, ib, sb_, nb = blocks(f[:, :, :]), blocks(f_in[:, :, :]), blocks(f_first[:, :, :]), blocks(f_next[:, :, :])
                        nc.vector.tensor_copy(ib[:, :, 1:BW], fb[:, :, 1:BW]).then_inc(hg_dve.mark("f_in"), 1)
                        nc.vector.tensor_copy(sb_[:, :, 0:1], fb[:, :, 0:1]).then_inc(hg_dve.mark("f_first"), 1)
                        nc.vector.tensor_copy(nb[:, :, 0:BW - 1], fb[:, :, 1:BW]).then_inc(hg_dve.mark("f_next"), 1)
                        own(hg_dve, l, "f_next")
                        for c in range(2):
                            nc.vector.tensor_tensor_scan(pre[:, c, :], f_in[:, c, :], f_first[:, c, :], 0.0, ALU.mult, ALU.add).then_inc(hg_dve.mark(f"pre{c}"), 1)
                        for c in range(2):
                            nc.vector.tensor_tensor_scan(kd[:, c, ::-1], f_next[:, c, ::-1], c_("ends")[:, ::-1], 0.0, ALU.mult, ALU.add).then_inc(hg_dve.mark(f"suf{c}"), 1)
                        own(hg_dve, l, "suf1")
                        for e in range(2):
                            STT(whole(qdm[:, e]), whole(q), cst[:, CONST["headmask"][0] + e:CONST["headmask"][0] + e + 1], whole(pre),
                                ALU.mult, ALU.mult).then_inc(hg_dve.mark(f"qd{e}"), 1)
                    elif name == "gg":
                        dve.wait_ge(hg_act.sem, hg_act.at(l, "sig_g"))
                        STT(whole(gg), bank_of(f"slab{S_HG}")[:, :], IWS, whole(gg), ALU.mult, ALU.mult).then_inc(hg_dve.mark("gg"), 1)
                    elif name.startswith("lag"):
                        d = int(name[3:])
                        w_ = BW - d
                        n = 2 * NB * w_
                        dve.wait_ge(hg_pe.sem, hg_pe.at(l, name))
                        bv = b[:, 0:n].rearrange("p (b w) -> p b w", w=w_)
                        ob, vb = blocks(o[:, :, :]), blocks(v[:, :, :])
                        if d == 0:
                            TTo(ob, bv, vb, ALU.mult).then_inc(hg_dve.mark("t0"), 1)
                        else:
                            tv = olag[:, d % 2, 0:n].rearrange("p (b w) -> p b w", w=w_)
                            TTo(tv, bv, vb[:, :, 0:w_], ALU.mult).then_inc(hg_dve.mark(f"t{d}"), 1)
                            own(hg_dve, l, f"t{d}")
                            if d == 11:
                                own(hg_dve, l, "oi11")
                            TTo(ob[:, :, d:BW], ob[:, :, d:BW], tv, ALU.add).then_inc(hg_dve.mark(f"o{d}"), 1)
                    elif name.startswith("ds"):
                        r = int(name[2:])
                        dve.wait_ge(hg_pe.sem, hg_pe.at(l, name))
                        for e in range(2):
                            bl = 2 * r + e
                            if bl == NB - 1:
                                continue
                            if bl > 0:
                                own(hg_dve, l, f"st{bl}1")
                            for c in range(2):
                                src = b[:, e * 256 + c * P:e * 256 + (c + 1) * P]
                                dst = st[:, bl + 1, c * P:(c + 1) * P]
                                if bl == 0:
                                    nc.vector.tensor_copy(dst, src).then_inc(hg_dve.mark(f"st1{c}"), 1)
                                else:
                                    STT(dst, st[:, bl, c * P:(c + 1) * P], pre[:, c, bl * BW + BW - 1:bl * BW + BW], src).then_inc(hg_dve.mark(f"st{bl + 1}{c}"), 1)
                    elif name == "inter":
                        own(hg_dve, l, "o10")
                        for r in range(2):
                            dve.wait_ge(hg_pe.sem, hg_pe.at(l, f"inter{r}"))
                            for e in range(2):
                                r0, b0 = e * HD, (1 if r == 0 else 0)
                                ov = o[r0:r0 + HD, :, :].rearrange("p c (b w) -> p c b w", w=BW)[:, :, 8 * r + b0:8 * r + 8, :]
                                iv = bank_of(f"inter{r}")[r0:r0 + HD, :].rearrange("p (c b e w) -> p c b e w", c=2, b=8, e=2)[:, :, b0:, e, :]
                                TTo(ov, ov, iv, ALU.add).then_inc(hg_dve.mark(f"oi{r}{e}"), 1)
                    elif name == "oss":
                        dve.wait_ge(hg_pe.sem, hg_pe.at(l, name))
                        nc.vector.tensor_scalar(o_ms[:, :], b[:, 0:8], 1.0 / HD, EPS, ALU.mult, ALU.add).then_inc(hg_dve.mark("o_ms"), 1)
                    elif name == "hgy":
                        dve.wait_ge(hg_pe.sem, hg_pe.at(l, "orT"))
                        TTo(osq, whole(o), bank_of("orT")[:, :], ALU.mult).then_inc(hg_dve.mark("on"), 1)
                        own(hg_dve, l, "on")
                        STT(osq, osq, m_("g_hg"), whole(gg), ALU.mult, ALU.mult).then_inc(hg_dve.mark("y"), 1)
                    elif name == "orx":
                        dve.wait_ge(hg_pool.sem, hg_pool.at(l, "o_rs"))
                        nc.vector.tensor_copy(orx.rearrange("p t (e d) -> p (t e) d", d=HD),
                                              o_rs[:, :].unsqueeze(2).to_broadcast([P, 8, HD])).then_inc(hg_dve.mark("orx"), 1)
                    elif name == "hglo":
                        low_of(None, hg_dve, hg_act, 0)
                    elif name == "lat_ms":
                        dve.wait_ge(la_pe.sem, la_pe.at(l, "lat_ss"))
                        bs = bank_of("lat_ss")
                        nc.vector.tensor_scalar(lat_ms[:, 0:2], bs[:, 0:2], 1.0 / 256, EPS, ALU.mult, ALU.add).then_inc(la_dve.mark("lat_ms0"), 1)
                        nc.vector.tensor_scalar(lat_ms[:, 2:4], bs[:, 2:4], 1.0 / 128, EPS, ALU.mult, ALU.add).then_inc(la_dve.mark("lat_ms1"), 1)
                    elif name == "qk_ms":
                        dve.wait_ge(la_pool.sem, la_pool.at(l, "qksq"))
                        nc.vector.tensor_reduce(qk_ss[:, :], qksq[:, :, :], AX.X, ALU.add).then_inc(la_dve.mark("qk_ss"), 1)
                        own(la_dve, l, "qk_ss")
                        nc.vector.tensor_scalar(qk_ms[:, :], qk_ss[:, :], 1.0 / QK, EPS, ALU.mult, ALU.add).then_inc(la_dve.mark("qk_ms"), 1)
                    elif name == "s":
                        for h in range(NH):
                            dve.wait_ge(la_pe.sem, la_pe.at(l, f"s{h}"))
                            TTo(sc[:, h, :], bank_of(f"s{h}")[:, 0:384], c_("neg"), ALU.add).then_inc(la_dve.mark(f"sc{h}"), 1)
                        own(la_dve, l, "sc3")
                        nc.vector.tensor_reduce(mx[:, 0:4], sc[:, :, 0:P], AX.X, ALU.max).then_inc(la_dve.mark("mx0"), 1)
                        nc.vector.tensor_reduce(mx[:, 4:8], sc[:, :, P:384], AX.X, ALU.max).then_inc(la_dve.mark("mx1"), 1)
                        own(la_dve, l, "mx1")
                        nc.vector.tensor_scalar(nmx, mx, -(QK ** -0.5), None, ALU.mult).then_inc(la_dve.mark("nmx"), 1)
                    elif name == "rden":
                        dve.wait_ge(la_act.sem, la_act.at(l, "exp31"))
                        nc.vector.reciprocal(rden, den).then_inc(la_dve.mark("rden"), 1)
                    elif name == "lalo":
                        low_of(None, la_dve, la_act, 1)
                    elif name.startswith("taps"):
                        first, count = TAPS[name]
                        for tap in range(first, first + count):
                            for c in range(2):
                                wcol = m_("conv_w", c * CK + tap, 1)
                                if tap == 0:
                                    if c == 0:
                                        dve.wait_ge(cv_pool.sem, cv_pool.at(l, "u"))
                                    nc.vector.tensor_scalar(cacc[:, c, :], cu[:, c, 0:T], wcol, m_("conv_b", c, 1), ALU.mult, ALU.add).then_inc(cv_dve.mark(f"tap0{c}"), 1)
                                else:
                                    own(cv_dve, l, f"tap{tap - 1}{c}")
                                    STT(cacc[:, c, :], cu[:, c, tap:tap + T], wcol, cacc[:, c, :]).then_inc(cv_dve.mark(f"tap{tap}{c}"), 1)
                    elif name == "ln":
                        dve.wait_ge(cv_pe.sem, cv_pe.at(l, "lnT"))
                        b = bank_of("lnT")
                        for t in range(TT):
                            nc.vector.bn_stats(bnst[:, t, :], b[:, t * 256:(t + 1) * 256]).then_inc(cv_dve.mark(f"bs{t}"), 1)
                    elif name == "aggr":
                        for t in range(TT):
                            nc.vector.bn_aggr(ln_ag[:, 2 * t:2 * t + 2], bnst[:, t, :]).then_inc(cv_dve.mark(f"ag{t}"), 1)
                        own(cv_dve, l, "ag1")
                        nc.vector.tensor_scalar(ln_ms, ln_ag[:, 1:4:2], 1e-5, None, ALU.add).then_inc(cv_dve.mark("ln_ms"), 1)
                    elif name == "cn":
                        dve.wait_ge(cv_pool.sem, cv_pool.at(l, "ln_rs"))
                        for t in range(TT):
                            nc.vector.tensor_scalar(cn[:, t, :], bank_of("lnT")[:, t * 256:(t + 1) * 256], ln_ag[:, 2 * t:2 * t + 1], ln_rs[:, t:t + 1],
                                                    ALU.subtract, ALU.mult).then_inc(cv_dve.mark(f"cn{t}"), 1)
                    elif name == "cvlo":
                        low_of(None, cv_dve, cv_act, 2)
                    elif name.startswith("scan"):
                        h = int(name[4])
                        dve.wait_ge(sk_act.sem, sk_act.at(l, f"omb{h}"))
                        nc.vector.tensor_tensor_scan(incl[:, h * 384:(h + 1) * 384][:, ::-1], omb[:, h, ::-1], c_("ge")[:, ::-1], 1.0,
                                                     ALU.mult, ALU.max).then_inc(sk_dve.mark(name), 1)
                    elif name == "sklo":
                        low_of(None, sk_dve, sk_act, 3)
                    else:
                        raise ValueError(name)

                TAPS = {f"taps{i}": (4 * i, min(4, CK - 4 * i)) for i in range(8)}
                tasks = {0: ["q"], 1: ["f"], 3: ["gg"]}

                def put(n, *names):
                    tasks.setdefault(n, []).extend(names)

                put(9, "qk_ms")
                for d in range(BW):
                    put(4 + d, f"lag{d}")
                put(7, "lat_ms")
                for r in range(8):
                    put(10 + r // 2, f"ds{r}")
                for i in range(8):
                    put(8 + i, f"taps{i}")
                put(15, "scan0", "scan1", "scan2", "scan3")
                put(16, "s")
                put(18, "rden")
                put(14, "inter")
                put(19, "ln")
                put(20, "aggr", "cn")
                put(20, "sklo")
                put(21, "oss")
                put(22, "lalo")
                put(22, "orx")
                put(23, "hgy")
                put(24, "cvlo")
                put(25, "hglo")
                dve.wait_ge(mixp_in, l * 16 + 16)
                norm(l, 1, [0])
                for n in range(1, AHEAD):
                    split(n)
                nc.vector.tensor_scalar(gql[:, :], m_("g_latent"), IWS, None, ALU.mult).then_inc(la_dve.mark("gql"), 1)
                for n in range(S_BR):
                    if "aggr" in tasks.get(n, []):
                        own(cv_dve, l, "bs1")
                    split(n + AHEAD)
                    for name in tasks.get(n, []):
                        task(name)
                def merged_low(r):
                    dve.wait_ge(mg_act.sem, mg_act.at(l, f"hi{r}"))
                    sl = slice(2 * r, 2 * r + 2)
                    TTo(ml[:, sl, :].rearrange("p c t -> p (c t)"), mg[:, sl, :].rearrange("p c t -> p (c t)"),
                        mh[:, sl, :].rearrange("p c t -> p (c t)"), ALU.subtract).then_inc(mg_dve.mark(f"lo{r}"), 1)

                for i, br in enumerate(BRANCH_ORDER):
                    split(S_BR + i + AHEAD)
                    for r in range(4):
                        if r < 3:
                            dve.wait_ge(mg_pe.sem, mg_pe.at(l, f"br{i}{r}"))
                        else:
                            dve.wait_ge(slab_done, done_at(l, S_BR + i))
                        gt = gates[:, br, 2 * r:2 * r + 2, :].rearrange("p c t -> p (c t)")
                        bk = bank_of(f"br{i}{r}")[:, :]
                        if i == 0:
                            dst = mg[:, 2 * r:2 * r + 2, :].rearrange("p c t -> p (c t)")
                        else:
                            dst = mgtmp[:, r % 2, :]
                            if i == 3 and r >= 2:
                                own(mg_dve, l, f"a3{r - 2}")
                            elif i > 1 or r >= 2:
                                a_, b_ = (i, r - 2) if r >= 2 else (i - 1, r + 2)
                                dve.wait_ge(mg_pool.sem, mg_pool.at(l, f"a{a_}{b_}"))
                        if i == 0:
                            dve.wait_ge(mg_act.sem, mg_act.at(l, "gate15"))
                        STT(dst, bk, IWS, gt, ALU.mult, ALU.mult).then_inc(mg_dve.mark(f"m{i}{r}"), 1)
                        if i == 3:
                            m_r = mg[:, 2 * r:2 * r + 2, :].rearrange("p c t -> p (c t)")
                            dve.wait_ge(mg_pool.sem, mg_pool.at(l, f"a2{r}"))
                            own(mg_dve, l, f"m3{r}")
                            TTo(m_r, m_r, dst, ALU.add).then_inc(mg_dve.mark(f"a3{r}"), 1)
                            if r >= 1:
                                merged_low(r - 1)
                merged_low(3)

                def renew(l, n, what):
                    dve.wait_ge(slab_done, done_at(l, n))
                    for t in range(TT):
                        for e in range(2):
                            xs = xr[:, t, e * 512:(e + 1) * 512]
                            STT(xs, bank[4 + 2 * t + e][:, :], IWS, xs).then_inc(x_new, 1)

                for n in range(S_FF, S_FF + 5):
                    split(n)
                renew(l, S_WO + 3, "w_out")
                dve.wait_ge(ffp_in, l * 16 + 16)
                norm(l, 2, [])
                nc.vector.tensor_scalar(ftap[:, :], f_("w"), IWS, None, ALU.mult).then_inc(ff_tap, 1)

                def ff_step(j, jp):
                    for half, (u, nm) in enumerate(((u_v, "v"), (u_g, "g"))):
                        bk = bank[2 * jp + half]
                        for sh in (1, 2):
                            for c in range(2):
                                if sh == 1:
                                    if c == 0:
                                        dve.wait_ge(ff_act, ffa(l, j, f"{nm}1"))
                                else:
                                    dve.wait_ge(ff_dve, ffd(l, j, f"{nm}{c}a"))
                                STT(u[:, jp, c, sh:T], bk[:, c * T:(c + 1) * T - sh], tap_of(j, half, c, 2 - sh), u[:, jp, c, sh:T]).then_inc(ff_dve, 1)
                    uvf = u_v[:, jp, :, :].rearrange("p c t -> p (c t)")
                    dve.wait_ge(ff_act, ffa(l, j, "silu"))
                    dve.wait_ge(ff_dve, ffd(l, j, "g1b"))
                    TTo(uvf, u_g[:, jp, :, :].rearrange("p c t -> p (c t)"), uvf, ALU.mult).then_inc(ff_dve, 1)
                    dve.wait_ge(ff_act, ffa(l, j, "high"))
                    TTo(gl[:, jp, :, :].rearrange("p c t -> p (c t)"), uvf, gh[:, jp, :, :].rearrange("p c t -> p (c t)"),
                        ALU.subtract).then_inc(ff_dve, 1)

                ff_step(0, 0)
                for n in range(S_FF + 5, S_FF + 8):
                    split(n)
                ff_step(1, 1)
                with dve.Fori(0, (J - 3) // 2) as i:
                    for e in range(2):
                        for m in range(3):
                            n0 = S_FF + 8 + 3 * e + m
                            split_at(i * 6 + n0, n0 % RING, n0 % RAW)
                        ff_step(i * 2 + (2 + e), e)
                n_next = S_FF + 8 + 24
                assert n_next == NSLAB - 1
                split(NSLAB - 1)
                ff_step(J - 1, 0)
                renew(l, NSLAB - 1, "down")

        @block.gpsimd
        def _(pool):
            nc.gpsimd.memset(cu[:, :, 0:CK - 1], 0.0).then_inc(pool_setup, 1)
            pool.wait_ge(const_in, 16)

            def power(out_, in_, n):
                mh_ = c_("minushalf")
                return nc.gpsimd.tensor_tensor(out_, in_, mh_.to_broadcast([P, n]) if n > 1 else mh_, ALU.pow)

            def TTo(out_, a, b, op):
                return nc.gpsimd.tensor_tensor(out_, a, b, op)

            def whole(ap2):
                return ap2[:, :, :].rearrange("p c t -> p (c t)")

            def own(s_, l, step):
                pool.wait_ge(s_.sem, s_.at(l, step))

            with pool.Fori(0, L) as l:
                def rsqrt_norm(w):
                    for t in range(TT):
                        pool.wait_ge(nm_dve.sem, nm_dve.at(l, f"{w}ms{t}"))
                        power(rs[:, t:t + 1], ms[:, t:t + 1], 1).then_inc(nm_pool.mark(f"{w}rs{t}"), 1)

                def lag(d):
                    w_ = BW - d
                    n = 2 * NB * w_
                    qb, kb, fb, wb = (blocks(t_[:, :, :]) for t_ in (q, k, f, wlag))
                    if d == 1:
                        TTo(wb[:, :, 1:BW], qb[:, :, 1:BW], fb[:, :, 1:BW], ALU.mult).then_inc(hg_pool.mark("w1"), 1)
                    elif d > 1:
                        own(hg_pool, l, f"p{d - 1}")
                        TTo(wb[:, :, d:BW], wb[:, :, d:BW], fb[:, :, 1:BW - d + 1], ALU.mult).then_inc(hg_pool.mark(f"w{d}"), 1)
                    if d >= 1:
                        own(hg_pool, l, f"w{d}")
                    if d >= 2:
                        pool.wait_ge(hg_pe.sem, hg_pe.at(l, f"lag{d - 2}"))
                    src = qb if d == 0 else wb
                    TTo(plag[:, d % 2, 0:n].rearrange("p (b w) -> p b w", w=w_), src[:, :, d:BW], kb[:, :, 0:w_],
                        ALU.mult).then_inc(hg_pool.mark(f"p{d}"), 1)

                rsqrt_norm(1)
                nc.gpsimd.memset(view(g0, 0, 1536), 0.0).then_inc(hg_pool.mark("zero"), 1)
                pool.wait_ge(hg_dve.sem, hg_dve.at(l, "suf1"))
                TTo(whole(kd), whole(k), whole(kd), ALU.mult).then_inc(hg_pool.mark("kd"), 1)
                lag(0)
                lag(1)
                lag(2)
                lag(3)
                pool.wait_ge(la_act.sem, la_act.at(l, "kr"))
                qk4 = qk[:, :, :].rearrange("p (a t h) c -> p a t h c", a=2, t=TT)
                pool.wait_ge(la_dve.sem, la_dve.at(l, "lat_ms1"))
                power(lat_rs, lat_ms, 4).then_inc(la_pool.mark("lat_rs"), 1)
                lag(4)
                pool.wait_ge(cv_act.sem, cv_act.at(l, "sg"))
                TTo(cu[:, :, CK - 1:], ca[:, :, :], sg_c[:, :, :], ALU.mult).then_inc(cv_pool.mark("u"), 1)
                for t in range(TT):
                    nc.gpsimd.tensor_copy(qk4[:, 1, t, :, NOPE:QK], kr[:, t:t + 1, :].to_broadcast([P, NH, ROPE])).then_inc(la_pool.mark(f"kr{t}"), 1)
                lag(5)
                pool.wait_ge(la_act.sem, la_act.at(l, "vm1"))
                own(la_pool, l, "kr1")
                TTo(whole(qksq), whole(qk), whole(qk), ALU.mult).then_inc(la_pool.mark("qksq"), 1)
                lag(6)
                pool.wait_ge(la_dve.sem, la_dve.at(l, "qk_ms"))
                power(qk_rs[:, :], qk_ms[:, :], 16).then_inc(la_pool.mark("qk_rs"), 1)
                own(la_pool, l, "qk_rs")
                TTo(qk[:, :, :], qk[:, :, :], qk_rs[:, :].unsqueeze(2).to_broadcast([P, 16, QK]), ALU.mult).then_inc(la_pool.mark("qkn"), 1)
                own(la_pool, l, "qkn")
                lag(7)
                for a in range(2):
                    TTo(qk[:, 8 * a:8 * a + 8, :], qk[:, 8 * a:8 * a + 8, :], m_("g_qk", a * QK, QK).unsqueeze(1).to_broadcast([P, 8, QK]),
                        ALU.mult).then_inc(la_pool.mark(f"qkg{a}"), 1)
                lag(8)
                own(la_pool, l, "qkg1")
                x1, x2 = qk[:, :, NOPE:NOPE + 16], qk[:, :, NOPE + 16:QK]
                for a in range(2):
                    half = slice(8 * a, 8 * a + 8)
                    for i_, (x_, tab) in enumerate(((x1, "cos"), (x2, "sin"), (x2, "cos"), (x1, "sin"))):
                        tv = c_(tab).rearrange("p (t r) -> p t r", t=TT).unsqueeze(2).to_broadcast([P, TT, NH, 16])
                        TTo(rt[:, i_, half, :].rearrange("p (t h) r -> p t h r", t=TT), x_[:, half, :].rearrange("p (t h) r -> p t h r", t=TT),
                            tv, ALU.mult).then_inc(la_pool.mark(f"rot_{a}{i_}"), 1)
                own(la_pool, l, "rot_13")
                TTo(x1, rt[:, 0, :, :], rt[:, 1, :, :], ALU.subtract).then_inc(la_pool.mark("rot2"), 1)
                TTo(x2, rt[:, 2, :, :], rt[:, 3, :, :], ALU.add).then_inc(la_pool.mark("rot3"), 1)
                for d in range(9, 13):
                    lag(d)
                pool.wait_ge(sk_act.sem, sk_act.at(l, "omb3"))
                lag(13)
                nc.gpsimd.memset(incl[:, NH * 384:NH * 384 + 1], 1.0).then_inc(sk_pool.mark("end"), 1)
                own(sk_pool, l, "end")
                lag(14)
                pool.wait_ge(sk_dve.sem, sk_dve.at(l, "scan3"))
                TTo(whole(beta), whole(beta), incl[:, 1:NH * 384 + 1], ALU.mult).then_inc(sk_pool.mark("w1"), 1)
                own(sk_pool, l, "w1")
                TTo(beta[:, :, :], beta[:, :, :], c_("lt").unsqueeze(1).to_broadcast([P, NH, 384]), ALU.mult).then_inc(sk_pool.mark("w2"), 1)
                lag(15)
                pool.wait_ge(la_dve.sem, la_dve.at(l, "rden"))
                TTo(pr[:, :, 0:P], pr[:, :, 0:P], rden[:, 0:4].unsqueeze(2).to_broadcast([P, NH, P]), ALU.mult).then_inc(la_pool.mark("pn0"), 1)
                TTo(pr[:, :, P:384], pr[:, :, P:384], rden[:, 4:8].unsqueeze(2).to_broadcast([P, NH, T]), ALU.mult).then_inc(la_pool.mark("pn1"), 1)
                pool.wait_ge(cv_dve.sem, cv_dve.at(l, "ln_ms"))
                power(ln_rs, ln_ms, 2).then_inc(cv_pool.mark("ln_rs"), 1)
                pool.wait_ge(hg_dve.sem, hg_dve.at(l, "o_ms"))
                power(o_rs[:, :], o_ms[:, :], 8).then_inc(hg_pool.mark("o_rs"), 1)
                pool.wait_ge(cv_act.sem, cv_act.at(l, "sig1"))
                TTo(y32[2], whole(cz), whole(csig), ALU.mult).then_inc(cv_pool.mark("y"), 1)
                for i in range(1, 3):
                    for r in range(4):
                        pool.wait_ge(mg_dve.sem, mg_dve.at(l, f"m{i}{r}"))
                        if i >= 2:
                            own(mg_pool, l, f"a{i - 1}{r}")
                        d_ = mg[:, 2 * r:2 * r + 2, :].rearrange("p c t -> p (c t)")
                        TTo(d_, d_, mgtmp[:, r % 2, :], ALU.add).then_inc(mg_pool.mark(f"a{i}{r}"), 1)
                rsqrt_norm(2)


def last_in_slot(slot, slots):
    return max(n for n in range(NSLAB) if n % slots == slot)


PER_SLOT = [sum(1 for n in range(NSLAB) if n % RAW == s) for s in range(RAW)]


def constants():
    c = np.zeros((P, NCONST), np.float32)
    p = np.arange(P)

    def put(name, a):
        c[:, CONST[name][0]:CONST[name][1]] = a

    put("ident", np.eye(P))
    put("headones", (p[:, None] // HD) == (p[None, :] // HD))
    put("blk8", (p[:, None] // BW) == np.arange(8)[None, :])
    put("ends", np.broadcast_to(np.arange(T) % BW == BW - 1, (P, T)))
    put("headmask", (p[:, None] // HD) == np.arange(2)[None, :])
    below = np.concatenate([p[None, :] < p[:, None], np.ones((P, P), bool), p[None, :] < p[:, None]], 1)
    upto = np.concatenate([p[None, :] <= p[:, None], np.ones((P, P), bool), p[None, :] <= p[:, None]], 1)
    put("neg", np.where(upto, 0.0, -1e30))
    put("ge", ~below)
    put("lt", below)
    half = ROPE // 2
    freqs = (np.float32(10000.0) ** (-np.arange(half, dtype=np.float32) / np.float32(half))).astype(np.float32)
    ang = (np.arange(T, dtype=np.float32)[:, None] * freqs[None, :]).astype(np.float32)
    for name, fn in (("cos", np.cos), ("sin", np.sin)):
        tab = fn(ang).astype(np.float32).reshape(TT, P, half).transpose(1, 0, 2)
        put(name, tab.reshape(P, -1))
    put("one", 1.0)
    put("minushalf", -0.5)
    return c


def lay_out(a):
    slabs = np.zeros((L, NSLAB, P, SLAB), np.float32)

    def cols(w, c0, n):
        s = np.zeros((P, KT, 256), np.float32)
        s[:, :, :n] = w[:, c0:c0 + n].reshape(KT, P, n).transpose(1, 0, 2)
        return s.reshape(P, SLAB)

    def rows(w, r0):
        return w[r0:r0 + 256].reshape(2, P, D).transpose(1, 0, 2).reshape(P, SLAB)

    for l in range(L):
        for n, (c0, w) in enumerate(PROJ):
            slabs[l, n] = cols(a["w_in"][l], c0, w)
        for g in range(16):
            slabs[l, S_GATE + g] = cols(a["w_in"][l], GATE0 + (g // 4) * D + (g % 4) * 256, 256)
        for i, br in enumerate(BRANCH_ORDER):
            slabs[l, S_BR + i] = rows(a["w_branch"][l, br], 0)
        for s in range(4):
            slabs[l, S_WO + s] = rows(a["w_out"][l], 256 * s)
        for j in range(J):
            slabs[l, slab_v(j)] = cols(a["w_up"][l], 256 * j, 256)
            slabs[l, slab_g(j)] = cols(a["w_up"][l], FF + 256 * j, 256)
            slabs[l, slab_d(j)] = rows(a["w_down"][l], 256 * j)

    def per_tile(v, n):
        return v.reshape(n, P).T

    mp = np.zeros((L, P, NMIXP), np.float32)
    fp = np.zeros((L, P, NFFP), np.float32)
    wup = np.zeros((L, P, NWU), np.float32)
    for l in range(L):
        def put(name, v):
            mp[l, :, MIXP[name][0]:MIXP[name][1]] = v
        put("g_mix", per_tile(a["g_mix"][l], KT))
        put("g_hg", np.concatenate([a["g_hg_out"][l]] * 2)[:, None])
        put("g_latent", np.concatenate([per_tile(a["g_q_lat"][l], 2), per_tile(a["g_kv_lat"][l], 1)], 1))
        put("g_qk", np.broadcast_to(np.concatenate([a["g_qk_q"][l], a["g_qk_k"][l]])[None], (P, 2 * QK)))
        put("conv_w", a["conv_w"][l].reshape(CK, 2, P).transpose(2, 1, 0).reshape(P, -1))
        put("conv_b", per_tile(a["conv_b"][l], 2))
        put("ln_g", per_tile(a["conv_ln_g"][l], 2))
        put("ln_b", per_tile(a["conv_ln_b"][l], 2))
        wup[l] = np.concatenate([a["w_uq"][l].reshape(2, P, NH * QK).transpose(1, 0, 2).reshape(P, -1), a["w_ukv"][l]], 1)

        def putf(name, v):
            fp[l, :, FFP[name][0]:FFP[name][1]] = v
        putf("g_ffn", per_tile(a["g_ffn"][l], KT))
        putf("w", a["ffn_conv_w"][l].reshape(3, 2, J, 2, P).transpose(4, 2, 1, 3, 0).reshape(P, -1))
        putf("b", a["ffn_conv_b"][l].reshape(2, J, 2, P).transpose(3, 1, 0, 2).reshape(P, -1))
    lbl = a["lb_logits"].reshape(L, 2, P).transpose(2, 0, 1).reshape(P, 2 * L)
    return {"x": np.ascontiguousarray(a["x"][0]), "slabs": slabs, "lb_logits": np.ascontiguousarray(lbl),
            "consts": constants(), "mixp": mp, "wup": wup, "ffp": fp}


def kernel(**inputs):
    import concourse.bacc as bacc
    from concourse.bass_utils import run_bass_kernel_spmd

    arrays = lay_out({n: np.asarray(v) for n, v in inputs.items()})
    book = {}
    for _ in range(2):
        nc = bacc.Bacc("TRN2", target_bir_lowering=False, num_devices=1)
        args = [nc.dram_tensor(f"in_{n}", v.shape, mybir.dt.from_np(v.dtype), kind="ExternalInput").ap() for n, v in arrays.items()]
        args.append(nc.dram_tensor("out_0", (T, D), mybir.dt.float32, kind="ExternalOutput").ap())
        program(nc, book, *args)
    r = run_bass_kernel_spmd(nc, [{f"in_{n}": v for n, v in arrays.items()}], core_ids=[0])
    return r.results[0]["out_0"].reshape(1, T, D)
```

```python
from contextlib import ExitStack

import numpy as np
import concourse.bass as bass
from concourse import mybir

F32 = mybir.dt.float32
F16 = mybir.dt.float16
ALU = mybir.AluOpType
ACT = mybir.ActivationFunctionType
AX = mybir.AxisListType

P = 128
L = 2
T = 256
D = 1024
KT = D // P
TT = T // P
NH = 4
HD = 64
NOPE, ROPE = 64, 32
QK = NOPE + ROPE
CK = 31
FF = 2816
J = FF // 256
BW = 16
NB = T // BW
EPS = 1e-6
RAW = 3
RING = 6
WS = 64.0
IWS = 1.0 / WS
SLAB = 2048
START = 1
INTER_AT = 12
AHEAD = 4

PROJ = [(0, 256), (256, 256), (512, 256), (768, 256), (1024, 256), (1280, 160),
        (1440, 256), (1696, 256), (1952, 256), (2208, 256), (2464, 256)]
S_HQ, S_HF, S_HV, S_HG, S_CQ, S_KV, S_CA, S_CG, S_SQ, S_SK, S_SV = range(11)
S_GATE = len(PROJ)
S_BR = S_GATE + 16
S_WO = S_BR + 4
S_FF = S_WO + 4
NSLAB = S_FF + 3 * J
GATE0 = 2720
GATE_ORDER = [0, 1, 3, 2]
BRANCH_ORDER = [3, 2, 1, 0]


def slab_v(j):
    return S_FF + 3 * j - 1 if not (isinstance(j, int) and j == 0) else S_FF


def slab_g(j):
    return slab_v(j) + 1


def slab_d(j):
    return S_FF + 3 * j + 4 if not (isinstance(j, int) and j == J - 1) else S_FF + 3 * J - 1


CONST = {}
MIXP = {}
FFP = {}


def columns(table, spec):
    at = 0
    for name, width in spec:
        table[name] = (at, at + width)
        at += width
    return at


NCONST = columns(CONST, [("ident", P), ("one", 1), ("minushalf", 1),
                         ("headones", P), ("blk8", 8), ("ends", T), ("headmask", 2),
                         ("neg", 384), ("ge", 384), ("lt", 384), ("cos", 32), ("sin", 32)])
NFIRST = CONST["minushalf"][1]
NMIXP = columns(MIXP, [("g_mix", KT), ("g_hg", 1), ("g_latent", 3), ("g_qk", 2 * QK),
                       ("conv_w", 2 * CK), ("conv_b", 2), ("ln_g", 2), ("ln_b", 2)])
NWU = 2 * NH * QK + NH * 128
NFFP = columns(FFP, [("g_ffn", KT), ("w", 3 * 2 * J * 2), ("b", 2 * J * 2)])


class Steps:

    def __init__(self, book, sem, name, start=0):
        self.sem, self.order, self.start = sem, [], start
        self.known = book.get(name, [])
        book[name] = self.order

    def mark(self, step):
        self.order.append(step)
        return self.sem

    def total(self, l):
        return l * len(self.known) + self.start

    def at(self, l, step):
        if step not in self.known:
            return 1
        return l * len(self.known) + (self.known.index(step) + 1 + self.start)


def program(nc, book, x, slabs, lb_logits, consts, mixp, wup, ffp, out):
    ctx = ExitStack()
    with ctx:
        def sb(name, shape, dt=F32):
            return ctx.enter_context(nc.sbuf_tensor(name, [P] + shape, dt))

        def sem(name):
            return ctx.enter_context(nc.semaphore(name))

        def steps(name, start=0):
            return Steps(book, sem(name), name, start)

        wf = sb("wf", [RAW, SLAB])
        wh = sb("wh", [RING, SLAB], F16)
        wl = sb("wl", [RING, SLAB], F16)
        xr = sb("xr", [TT, D])
        xn = sb("xn", [TT, D])
        hh = sb("hh", [KT, T], F16)
        hl = sb("hl", [KT, T], F16)
        h32 = sb("h32", [2, 2 * T])
        gates = sb("gates", [4, KT, T])
        mgtmp = sb("mgtmp", [2, 2 * T])
        fx = sb("fx", [4112])

        def view(tensor2, at, *dims):
            n = int(np.prod(dims))
            v_ = tensor2[:, at:at + n]
            names = " ".join("abcd"[:len(dims)])
            sizes = {x_: d_ for x_, d_ in zip("abcd", dims)}
            return v_.rearrange(f"p ({names}) -> p {names}", **sizes) if len(dims) > 1 else v_

        g0, g1, g2, g3 = (gates[:, b_, :, :].rearrange("p k t -> p (k t)") for b_ in range(4))
        g23 = gates[:, 2:4, :, :].rearrange("p b k t -> p (b k t)")
        xflat = xn[:, :, :].rearrange("p t d -> p (t d)")
        mg = view(xflat, 0, KT, T)
        mh, ml = hh, hl
        yh = sb("yh", [4, 2, T], F16)
        yl = sb("yl", [4, 2, T], F16)
        cst = sb("cst", [NCONST])
        pm = sb("pm", [NMIXP])
        pf = sb("pf", [NFFP])
        gql = sb("gql", [3])
        ftap = sb("ftap", [12 * J])
        stat = sb("stat", [64])
        idle = sb("idle", [P], F16)

        def c_(name):
            return cst[:, CONST[name][0]:CONST[name][1]]

        def m_(name, a=0, n=None):
            lo, hi = MIXP[name]
            return pm[:, lo + a:(hi if n is None else lo + a + n)]

        def f_(name, a=0, n=None):
            lo, hi = FFP[name]
            return pf[:, lo + a:(hi if n is None else lo + a + n)]

        ident, headones = c_("ident"), c_("headones")

        ss, ms, rs = sb("ss", [TT, 2]), stat[:, 2:4], stat[:, 4:6]
        ms0 = stat[:, 0:2]
        lat_ms, lat_rs = stat[:, 6:10], stat[:, 10:14]
        ln_ag, ln_ms, ln_rs = stat[:, 14:18], stat[:, 18:20], stat[:, 20:22]
        mx, nmx, den, rden = stat[:, 22:30], stat[:, 30:38], stat[:, 38:46], stat[:, 46:54]
        bnst = sb("bnst", [2, 6])
        qk_ss, qk_ms, qk_rs = sb("qk_ss", [16]), sb("qk_ms", [16]), sb("qk_rs", [16])
        lbx = sb("lbx", [8, 4])
        lbt, omlbt = sb("lbt", [L * 2]), sb("omlbt", [L * 2])
        lb, omlb = sb("lb", [2]), sb("omlb", [2])

        q, f, k, v, gg, o, pre, wlag = (sb(n, [2, T]) for n in ("q", "f", "k", "v", "gg", "o", "pre", "wlag"))
        f_in, f_first, f_next = view(g0, 0, 2, T), view(g0, 512, 2, T), view(g0, 1024, 2, T)
        kd = view(g0, 1536, 2, T)
        qdm = sb("qdm", [2, 2, T])
        plag = h32[:, :, :]
        olag = mgtmp[:, :, :]
        products = [mgtmp[:, 0, :], mgtmp[:, 1, :], h32[:, 0, :], h32[:, 1, :]]
        kdm = view(fx[:, :], 0, 8, TT * 256)
        vt = view(g1, 0, TT, 256)
        st = view(g23, 0, NB, 256)
        osq = view(fx[:, :], 1536, 2 * T)
        cqs, cqg = view(g1, 0, 2, T), view(g1, 512, 2, T)
        kvs, kvg = view(g1, 1024, T), view(g1, 1280, T)
        kr = view(g1, 1536, TT, ROPE)
        wu = view(g2, 0, NWU)
        qk = sb("qk", [16 * QK])
        prT = view(qk[:, :], 0, NH, 384)
        qk = view(qk[:, :], 0, 16, QK)
        qksq = view(xflat, 0, 16, QK)
        rt = view(xflat, 0, 4, 16, 16)
        vm = sb("vm", [TT, NH, HD])
        qkT = view(g3, 0, 2, NH, T)
        sc = view(xflat, 0, NH, 384)
        pr = sc
        sqT, skT = view(g1, 512, 2, T), view(g1, 1024, 2, T)
        sv = sb("sv", [TT, 256])
        beta = view(g2, 0, NH, 384)
        omb = view(fx[:, :], 0, NH, 384)
        wT = omb
        incl = view(fx[:, :], 1536, NH * 384 + 1)
        ca, sg_c = view(g0, 0, 2, T), view(g0, 512, 2, T)
        cu = sb("cu", [2, T + CK - 1])
        cacc = sb("cacc", [2, T])
        cn = view(fx[:, :], 3592, TT, 256)
        cz, csig = view(fx[:, :], 2048, 2, T), view(fx[:, :], 2560, 2, T)
        y32 = [osq, view(xflat, 1536, 2 * T), view(fx[:, :], 2048, 2 * T), view(fx[:, :], 3080, 2 * T)]
        orx = view(wlag[:, :, :].rearrange("p c t -> p (c t)"), 0, TT, 256)
        o_ms, o_rs = sb("o_ms", [8]), sb("o_rs", [8])
        u_v, u_g = view(fx[:, :], 0, 2, 2, T), view(fx[:, :], 1024, 2, 2, T)
        gh = view(fx[:, 2048:2560].bitcast(F16), 0, 2, 2, T)
        gl = view(fx[:, 2560:3072].bitcast(F16), 0, 2, 2, T)

        bank = [ctx.enter_context(nc.psum_tensor(f"bank{i}", [P, 512], F32)) for i in range(8)]

        first_in, const_in, logits_in, mixp_in, wu_in, ffp_in = (sem(n) for n in ("first_in", "const_in", "logits_in", "mixp_in", "wu_in", "ffp_in"))
        x_in = [sem(f"x_in{t}") for t in range(TT)]
        slab_in = [sem(f"slab_in{i}") for i in range(RAW)]
        high_ready = sem("high_ready")
        low_ready = sem("low_ready")
        slab_done = sem("slab_done")
        half_done = sem("half_done")
        x_new = sem("x_new")
        setup = sem("setup")
        setup_act = sem("setup_act")
        pool_setup = sem("pool_setup")
        out_done = sem("out_done")
        nm_pe, nm_act, nm_dve, nm_pool = (steps(f"norm_{e}") for e in ("pe", "act", "dve", "pool"))
        hg_pe, hg_act, hg_dve, hg_pool = (steps(f"hgrn_{e}") for e in ("pe", "act", "dve", "pool"))
        la_pe, la_act, la_dve, la_pool = (steps(f"latent_{e}") for e in ("pe", "act", "dve", "pool"))
        cv_pe, cv_act, cv_dve, cv_pool = (steps(f"conv_{e}") for e in ("pe", "act", "dve", "pool"))
        sk_pe, sk_act, sk_dve, sk_pool = (steps(f"stick_{e}") for e in ("pe", "act", "dve", "pool"))
        mg_pe, mg_act, mg_pool = (steps(f"merge_{e}") for e in ("pe", "act", "pool"))
        mg_dve = steps("merge_dve", START)
        ff_act, ff_dve = sem("ffn_act"), sem("ffn_dve")
        ff_tap = sem("ffn_taps_scaled")

        FA = ["v0", "v1", "g0", "g1", "silu", "high"]
        FD = ["v0a", "v1a", "v0b", "v1b", "g0a", "g1a", "g0b", "g1b", "mul", "low"]

        def ffa(l, j, step):
            return l * (J * len(FA)) + j * len(FA) + (FA.index(step) + 1)

        def ffd(l, j, step):
            return l * (J * len(FD)) + j * len(FD) + (FD.index(step) + 1 + START)

        def x_at(l, n):
            return l * 8 + (n + 4)

        def slab_at(l, n):
            return l * NSLAB + (n + 1)

        def low_at(l, n):
            return l * NSLAB + (n + 1 + RAW)

        def done_at(l, n):
            return l * NSLAB + (n + 1 + RING)

        uses = {}
        last_use = {}
        ring_at = [0]

        def use(name, reader, label, banks=6, where=None):
            b = where if where is not None else ring_at[0] % banks
            if where is None:
                ring_at[0] += 1
            uses[name] = (b, last_use.get(b))
            last_use[b] = (reader, label)

        for kp in range(4):
            use(f"n1{kp}", nm_dve, f"1lo{kp}")
        proj_reader = {S_HQ: (hg_dve, "q"), S_HF: (hg_act, "smf"), S_HV: (hg_act, "v"), S_HG: (hg_dve, "gg"),
                       S_CQ: (la_act, "cqg1"), S_KV: (la_act, "kr"), S_CA: (cv_act, "ca"),
                       S_CG: (cv_act, "sg"), S_SQ: (sk_act, "sq"), S_SK: (sk_act, "sk"), S_SV: (sk_act, "sv")}
        pieces = {}

        def after(n, *names):
            pieces.setdefault(n, []).extend(names)

        for d in range(BW):
            after(4 + d, f"lag{d}")
        after(7, "lat_ss", "lat_q0", "lat_q1", "lat_kv0", "lat_kv1")
        after(8, "kdT", "vT")
        for r in range(8):
            after(10 + r // 2, f"ds{r}")
        for i in range(4):
            after(INTER_AT + i, f"inter{i}")
        after(15, "z0", "z1", "z2", "z3")
        after(16, "qkT0", "qkT1", "qkT2", "qkT3")
        after(17, "s0", "s1", "s2", "s3")
        after(19, "wT0", "wT1", "wT2", "wT3")
        after(21, "skv", "oss", "lnT")
        after(22, "pT0", "pT1", "pT2", "pT3")
        after(23, "lav")
        after(24, "lnB")
        after(23, "orT")
        small_reader = {"lat_ss": (la_dve, "lat_ms1"), "lat_q0": (la_act, "q0"), "lat_q1": (la_act, "q1"),
                        "lat_kv0": (la_act, "vm0"), "lat_kv1": (la_act, "vm1"), "kdT": (hg_act, "kdm7"), "vT": (hg_act, "vt"),
                        "lnT": (cv_dve, "cn1"), "lnB": (cv_act, "sig1"),
                        "skv": (sk_act, "y"), "lav": (la_act, "y"), "oss": (hg_dve, "o_ms"), "orT": (hg_dve, "on")}
        for d in range(BW):
            small_reader[f"lag{d}"] = (hg_dve, f"t{d}")
        for r in range(8):
            small_reader[f"ds{r}"] = (hg_dve, f"st{min(2 * r + 2, NB - 1)}1")
        for i in range(4):
            small_reader[f"inter{i}"] = (hg_dve, f"oi{i}1")
        for h in range(4):
            small_reader[f"z{h}"] = (sk_act, f"omb{h}")
            small_reader[f"qkT{h}"] = (la_act, f"qkT{h}")
            small_reader[f"s{h}"] = (la_dve, f"sc{h}")
            small_reader[f"wT{h}"] = (sk_act, f"wT{h}")
            small_reader[f"pT{h}"] = (la_act, f"pT{h}")
        for n in range(S_BR):
            use(f"slab{n}", *(proj_reader[n] if n < S_GATE else (mg_act, f"gate{n - S_GATE}")))
            for name in pieces.get(n, []):
                if name.startswith("lag"):
                    use(name, *small_reader[name], where=6 + int(name[3:]) % 2)
                else:
                    use(name, *small_reader[name])
        for i in range(4):
            for r in range(4):
                use(f"br{i}{r}", mg_dve, f"m{i}{r}")
        for a in range(4):
            uses[f"wo{a}"] = (4 + a, last_use.get(4 + a))
            last_use[4 + a] = None
        for t in range(TT):
            for half in range(2):
                use(f"n2{t}{half}", nm_dve, f"2lo{t}{2 * half + 1}", where=2 + 2 * t + half)

        def bank_of(name):
            return bank[uses[name][0]]

        def wait_bank(eng, l, name):
            before = uses[name][1]
            if before is not None:
                eng.wait_ge(before[0].sem, before[0].at(l, before[1]))

        def blocks(ap2):
            return ap2.rearrange("p c (b w) -> p (c b) w", w=BW)

        def tap_of(j, half, c, tap):
            lo = (half * 2 + c) * 3 + tap
            return ftap[:, lo + j * 12:lo + j * 12 + 1] if isinstance(j, int) else ftap[:, bass.ds(j * 12 + lo, 1)]

        def bias_of(j, half, c):
            lo = FFP["b"][0] + half * 2 + c
            return pf[:, lo + j * 4:lo + j * 4 + 1] if isinstance(j, int) else pf[:, bass.ds(j * 4 + lo, 1)]

        block = ctx.enter_context(nc.Block())

        @block.sync
        def _(sp):
            sp.dma_start(lbx[:, 0, :], lb_logits).then_inc(logits_in, 16)
            for t in range(TT):
                sp.dma_start(xr[:, t, :], x[t * P:(t + 1) * P, :]).then_inc(x_in[t], 16)
                if t == 0:
                    sp.dma_start(cst[:, 0:NFIRST], consts[:, 0:NFIRST]).then_inc(first_in, 16)
            with sp.Fori(0, L) as l:
                sp.wait_ge(mg_dve.sem, mg_dve.total(l))
                sp.wait_ge(low_ready, low_at(l, last_in_slot(0, RAW) - NSLAB))

                def load(n, slot):
                    sp.dma_start(wf[:, slot, :], slabs[l, n, :, :]).then_inc(slab_in[slot], 16)

                load(0, 0)
                sp.dma_start(pm[:, :], mixp[l, :, :]).then_inc(mixp_in, 16)
                sp.dma_start(cst[:, NFIRST:], consts[:, NFIRST:]).then_inc(const_in, 16)
                for n in range(1, S_FF + 5):
                    sp.wait_ge(low_ready, low_at(l, n - RAW if n >= RAW else last_in_slot(n, RAW) - NSLAB))
                    load(n, n % RAW)
                    if n == RAW:
                        sp.dma_start(wu, wup[l, :, :]).then_inc(wu_in, 16)
                    if n == 11:
                        sp.wait_ge(ff_dve, l * (J * len(FD)) + START)
                        sp.dma_start(pf[:, :], ffp[l, :, :]).then_inc(ffp_in, 16)
                with sp.Fori(0, 4) as i:
                    for m in range(6):
                        n = i * 6 + (S_FF + 5 + m)
                        sp.wait_ge(low_ready, low_at(l, i * 6 + (S_FF + 5 + m - RAW)))
                        load(n, (S_FF + 5 + m) % RAW)
                for n in range(S_FF + 29, NSLAB):
                    sp.wait_ge(low_ready, low_at(l, n - RAW))
                    load(n, n % RAW)
            for t in range(TT):
                sp.wait_ge(x_new, x_at(L, 2 * t - 2))
                sp.dma_start(out[t * P:(t + 1) * P, :], xr[:, t, :]).then_inc(out_done, 16)
            sp.wait_ge(out_done, 16 * TT)

        @block.tensor
        def _(pe):
            pe.sem_inc(slab_done, RING)
            pe.wait_ge(pool_setup, 2)

            def mm3(o_, wt_h, wt_l, a_h, a_l, first, last, stationary_weight):
                passes = ((wt_h, a_h), (wt_h, a_l), (wt_l, a_h))
                for i_, (w_, a_) in enumerate(passes):
                    lt, rh = (w_, a_) if stationary_weight else (a_, w_)
                    ins = nc.tensor.matmul(o_, lt, rh, start=first and i_ == 0, stop=last and i_ == 2)
                return ins

            def mm(o_, lt, rh, first=True, last=True):
                return nc.tensor.matmul(o_, lt, rh, start=first, stop=last)

            def tr(o_, in_, n=P):
                return nc.tensor.transpose(o_, in_, ident)

            def keep_clock(n):
                for _ in range(n):
                    mm(bank[3][:, :], idle[:, :], idle[:, :].unsqueeze(1).to_broadcast([P, 4, P]))

            keep_clock(22)
            pe.wait_ge(first_in, 16)

            def norm_tile(l, t):
                for kp in range(4):
                    b = bank_of(f"n2{t}{kp // 2}")
                    if kp % 2 == 0:
                        wait_bank(pe, l, f"n2{t}{kp // 2}")
                        pe.wait_ge(nm_dve.sem, nm_dve.at(l, f"2xn{t}{kp // 2}"))
                    for c in range(2):
                        at = (kp % 2) * 256 + c * P
                        ins = tr(b[:, at:at + P], xn[:, t, (2 * kp + c) * P:(2 * kp + c + 1) * P])
                    if kp % 2 == 1:
                        ins.then_inc(nm_pe.mark(f"2T{t}{kp // 2}"), 1)

            def norm(l, w):
                wait_bank(pe, l, f"n{w}3")
                keep_clock(8)
                for t in range(TT):
                    for kp in range(4):
                        if kp % 2 == 0:
                            pe.wait_ge(nm_dve.sem, nm_dve.at(l, f"{w}xn{t}{kp // 2}"))
                        if t == 0:
                            wait_bank(pe, l, f"n{w}{kp}")
                        b = bank_of(f"n{w}{kp}")
                        for c in range(2):
                            ins = tr(b[:, c * T + t * P:c * T + t * P + P], xn[:, t, (2 * kp + c) * P:(2 * kp + c + 1) * P])
                        if t == TT - 1:
                            ins.then_inc(nm_pe.mark(f"{w}T{kp}"), 1)

            def column_slab(b, slot, chunks=2):
                for c in range(chunks):
                    for kt in range(KT):
                        a = kt * 256 + c * P
                        ins = mm3(b[:, c * T:(c + 1) * T], wh[:, slot, a:a + P], wl[:, slot, a:a + P],
                                  hh[:, kt, :], hl[:, kt, :], kt == 0, kt == KT - 1, True)
                return ins

            def pass_by_pass(b, slot, l, n, c, t0, width, high_x, low_x):
                for i_, (w_, a_) in enumerate(((wh, hh), (wl, hh), (wh, hl))):
                    if i_ == 0:
                        pe.wait_ge(high_ready, slab_at(l, n))
                    if i_ == 1:
                        pe.wait_ge(low_ready, low_at(l, n))
                    for kt in range(KT):
                        if i_ == 0 and kt % 2 == 0 and high_x is not None:
                            pe.wait_ge(nm_act.sem, nm_act.at(l, high_x(kt // 2)))
                        if i_ == 2 and kt % 2 == 0 and low_x is not None:
                            pe.wait_ge(nm_dve.sem, nm_dve.at(l, low_x(kt // 2)))
                        a = kt * 256 + c * P
                        ins = mm(b[:, c * T + t0:c * T + t0 + width], w_[:, slot, a:a + P], a_[:, kt, t0:t0 + width],
                                 i_ == 0 and kt == 0, i_ == 2 and kt == KT - 1)
                return ins

            def token_columns(b, slot, off, width, at):
                for t in range(TT):
                    for kt in range(KT):
                        a = kt * 256 + off
                        ins = mm3(b[:, at + t * width:at + (t + 1) * width], wh[:, slot, a:a + width],
                                  wl[:, slot, a:a + width], hh[:, kt, t * P:(t + 1) * P],
                                  hl[:, kt, t * P:(t + 1) * P], kt == 0, kt == KT - 1, False)
                return ins

            def row_slab(slot, ah, al, first, last, tiles=(0, 1)):
                for t in tiles:
                    for n in range(2):
                        for kt in range(2):
                            a = kt * D + n * 512
                            ins = mm3(bank[4 + 2 * t + n][:, :], wh[:, slot, a:a + 512], wl[:, slot, a:a + 512],
                                      ah[:, kt, t * P:(t + 1) * P], al[:, kt, t * P:(t + 1) * P],
                                      first and kt == 0, last and kt == 1, False)
                    if last and t == 0:
                        ins.then_inc(half_done, 1)
                return ins

            with pe.Fori(0, L) as l:
                norm(l, 1)

                def piece(name):
                    b = bank_of(name)
                    wait_bank(pe, l, name)
                    if name.startswith("lag"):
                        d = int(name[3:])
                        n = 2 * NB * (BW - d)
                        pe.wait_ge(hg_pool.sem, hg_pool.at(l, f"p{d}"))
                        mm(b[:, 0:n], headones, plag[:, d % 2, 0:n]).then_inc(hg_pe.mark(name), 1)
                    elif name == "lat_ss":
                        pe.wait_ge(la_act.sem, la_act.at(l, "kr"))
                        for t in range(TT):
                            for c in range(2):
                                mm(b[:, t:t + 1], cqs[:, c, t * P:(t + 1) * P], c_("one"), c == 0, c == 1)
                        for t in range(TT):
                            ins = mm(b[:, 2 + t:3 + t], kvs[:, t * P:(t + 1) * P], c_("one"))
                        ins.then_inc(la_pe.mark(name), 1)
                    elif name.startswith("lat_q"):
                        t = int(name[-1])
                        pe.wait_ge(wu_in, l * 16 + 16)
                        for c in range(2):
                            ins = mm(b[:, 0:NH * QK], cqg[:, c, t * P:(t + 1) * P], wu[:, c * NH * QK:(c + 1) * NH * QK], c == 0, c == 1)
                        ins.then_inc(la_pe.mark(name), 1)
                    elif name.startswith("lat_kv"):
                        t = int(name[-1])
                        mm(b[:, :], kvg[:, t * P:(t + 1) * P], wu[:, 2 * NH * QK:NWU]).then_inc(la_pe.mark(name), 1)
                    elif name == "kdT":
                        pe.wait_ge(hg_pool.sem, hg_pool.at(l, "kd"))
                        for t in range(TT):
                            for c in range(2):
                                ins = tr(b[:, t * 256 + c * P:t * 256 + (c + 1) * P], kd[:, c, t * P:(t + 1) * P])
                        ins.then_inc(hg_pe.mark(name), 1)
                    elif name == "vT":
                        for t in range(TT):
                            for c in range(2):
                                ins = tr(b[:, t * 256 + c * P:t * 256 + (c + 1) * P], v[:, c, t * P:(t + 1) * P])
                        ins.then_inc(hg_pe.mark(name), 1)
                    elif name.startswith("ds"):
                        r = int(name[2:])
                        if r == 0:
                            pe.wait_ge(hg_act.sem, hg_act.at(l, "vt"))
                        for e in range(2):
                            bl = 2 * r + e
                            if bl == NB - 1:
                                continue
                            t = bl // 8
                            for c in range(2):
                                ins = mm(b[:, e * 256 + c * P:e * 256 + (c + 1) * P],
                                         kdm[:, bl % 8, t * 256 + c * P:t * 256 + (c + 1) * P],
                                         vt[:, t, c * P:(c + 1) * P])
                        ins.then_inc(hg_pe.mark(name), 1)
                    elif name.startswith("inter"):
                        i_ = int(name[5])
                        pe.wait_ge(hg_dve.sem, hg_dve.at(l, f"st{4 * i_ + 3}1"))
                        for bl in range(max(1, 4 * i_), 4 * i_ + 4):
                            for c in range(2):
                                at = c * P + (bl % 4) * 2 * BW
                                ins = mm(b[:, at:at + 2 * BW], st[:, bl, c * P:(c + 1) * P], qdm[:, :, c, bl * BW:(bl + 1) * BW])
                        ins.then_inc(hg_pe.mark(name), 1)
                    elif name == "oss":
                        pe.wait_ge(hg_act.sem, hg_act.at(l, "osq"))
                        for t in range(TT):
                            for c in range(2):
                                ins = mm(b[:, t * 4 + c * 2:t * 4 + c * 2 + 2], osq[:, c * T + t * P:c * T + (t + 1) * P], c_("headmask"))
                        ins.then_inc(hg_pe.mark(name), 1)
                    elif name == "orT":
                        pe.wait_ge(hg_dve.sem, hg_dve.at(l, "orx"))
                        for c in range(2):
                            for t in range(TT):
                                ins = tr(b[:, c * T + t * P:c * T + (t + 1) * P], orx[:, t, c * P:(c + 1) * P])
                        ins.then_inc(hg_pe.mark(name), 1)
                    elif name[0] == "z":
                        h = int(name[1])
                        r0 = (h % 2) * HD
                        if h == 0:
                            pe.wait_ge(sk_act.sem, sk_act.at(l, "sv"))
                        mm(b[:, 0:P], sqT[r0:r0 + HD, h // 2, 0:P], skT[r0:r0 + HD, h // 2, 0:P])
                        mm(b[:, P:P + T], sqT[r0:r0 + HD, h // 2, P:T], skT[r0:r0 + HD, h // 2, :]).then_inc(sk_pe.mark(name), 1)
                    elif name.startswith("qkT"):
                        u = int(name[3])
                        if u == 0:
                            pe.wait_ge(la_pool.sem, la_pool.at(l, "rot3"))
                        for e in range(2):
                            for t in range(TT):
                                n = (u // 2) * 8 + t * 4 + (u % 2) * 2 + e
                                ins = nc.tensor.transpose(b[0:QK, e * T + t * P:e * T + (t + 1) * P], qk[:, n, :], ident)
                        ins.then_inc(la_pe.mark(name), 1)
                    elif name[0] == "s" and name[1].isdigit():
                        h = int(name[1])
                        if h == 0:
                            pe.wait_ge(la_act.sem, la_act.at(l, "qkT3"))
                        mm(b[:, 0:P], qkT[0:QK, 0, h, 0:P], qkT[0:QK, 1, h, 0:P])
                        mm(b[:, P:P + T], qkT[0:QK, 0, h, P:T], qkT[0:QK, 1, h, :]).then_inc(la_pe.mark(name), 1)
                    elif name.startswith("wT") or name.startswith("pT"):
                        h = int(name[2])
                        src = beta if name[0] == "w" else pr
                        if h == 0:
                            s_, lab = (sk_pool, "w2") if name[0] == "w" else (la_pool, "pn1")
                            pe.wait_ge(s_.sem, s_.at(l, lab))
                        for e in range(3):
                            ins = tr(b[:, e * P:(e + 1) * P], src[:, h, e * P:(e + 1) * P])
                        ins.then_inc((sk_pe if name[0] == "w" else la_pe).mark(name), 1)
                    elif name in ("skv", "lav"):
                        s_, pe_s, src = (sk_act, sk_pe, wT) if name == "skv" else (la_act, la_pe, prT)
                        pe.wait_ge(s_.sem, s_.at(l, "wT3" if name == "skv" else "pT3"))
                        for h in range(NH):
                            r0 = (h % 2) * HD
                            o_ = b[r0:r0 + HD, (h // 2) * T:(h // 2 + 1) * T]
                            vv = [sv[:, t, h * HD:(h + 1) * HD] if name == "skv" else vm[:, t, h, :] for t in range(TT)]
                            mm(o_[:, 0:P], vv[0], src[:, h, 0:P])
                            mm(o_[:, P:T], vv[0], src[:, h, P:2 * P], True, False)
                            ins = mm(o_[:, P:T], vv[1], src[:, h, 2 * P:3 * P], False, True)
                        ins.then_inc(pe_s.mark(name), 1)
                    elif name == "lnT":
                        pe.wait_ge(cv_dve.sem, cv_dve.at(l, f"tap{CK - 1}1"))
                        for t in range(TT):
                            for c in range(2):
                                ins = tr(b[:, t * 256 + c * P:t * 256 + (c + 1) * P], cacc[:, c, t * P:(t + 1) * P])
                        ins.then_inc(cv_pe.mark(name), 1)
                    elif name == "lnB":
                        pe.wait_ge(cv_dve.sem, cv_dve.at(l, "cn1"))
                        for c in range(2):
                            for t in range(TT):
                                ins = tr(b[:, c * T + t * P:c * T + (t + 1) * P], cn[:, t, c * P:(c + 1) * P])
                        ins.then_inc(cv_pe.mark(name), 1)
                    else:
                        raise ValueError(name)

                pe.wait_ge(const_in, l * 16 + 16)
                for n in range(S_BR):
                    if n > 0:
                        pe.wait_ge(low_ready, low_at(l, n))
                    wait_bank(pe, l, f"slab{n}")
                    b, slot = bank_of(f"slab{n}"), n % RING
                    if n == S_KV:
                        column_slab(b, slot, 1)
                        ins = token_columns(b, slot, P, ROPE, T)
                    elif n == S_SV:
                        ins = token_columns(b, slot, 0, 256, 0)
                    elif n == 0:
                        for c in range(2):
                            first = c == 0
                            ins = pass_by_pass(b, slot, l, n, c, 0, T, (lambda kp: f"1hi{kp}1") if first else None,
                                               (lambda kp: f"1lo{kp}") if first else None)
                    else:
                        ins = column_slab(b, slot)
                    ins.then_inc(slab_done, 1)
                    for name in pieces.get(n, []):
                        piece(name)
                ready = {3: (sk_dve, "lo"), 2: (cv_dve, "lo"), 1: (la_dve, "lo"), 0: (hg_dve, "lo")}
                for i, br in enumerate(BRANCH_ORDER):
                    n = S_BR + i
                    slot = n % RING
                    pe.wait_ge(low_ready, low_at(l, n))
                    pe.wait_ge(ready[br][0].sem, ready[br][0].at(l, ready[br][1]))
                    for r in range(4):
                        wait_bank(pe, l, f"br{i}{r}")
                        b = bank_of(f"br{i}{r}")
                        for c in range(2):
                            for kt in range(2):
                                a = kt * D + (2 * r + c) * P
                                ins = mm3(b[:, c * T:(c + 1) * T], wh[:, slot, a:a + P], wl[:, slot, a:a + P],
                                          yh[:, br, kt, :], yl[:, br, kt, :], kt == 0, kt == 1, True)
                        if r < 3:
                            ins.then_inc(mg_pe.mark(f"br{i}{r}"), 1)
                        else:
                            ins.then_inc(slab_done, 1)
                for a in range(4):
                    wait_bank(pe, l, f"wo{a}")
                for t in range(TT):
                    for s_ in range(4):
                        n = S_WO + s_
                        if t == 0:
                            pe.wait_ge(low_ready, low_at(l, n))
                            pe.wait_ge(mg_dve.sem, mg_dve.at(l, f"lo{s_}"))
                        ins = row_slab(n % RING, mh[:, 2 * s_:2 * s_ + 2, :], ml[:, 2 * s_:2 * s_ + 2, :],
                                       s_ == 0, s_ == 3, (t,))
                        if t == 1:
                            ins.then_inc(slab_done, 1)
                        if t == 1 and s_ == 2:
                            norm_tile(l, 0)

                def up_step(j, jp, slot_v, slot_g):
                    for half, n, slot in ((0, slab_v(j), slot_v), (1, slab_g(j), slot_g)):
                        pe.wait_ge(low_ready, low_at(l, n))
                        if not isinstance(j, int) or j >= 2:
                            pe.wait_ge(ff_dve, ffd(l, j - 2, "v1b" if half == 0 else "g1b"))
                        column_slab(bank[2 * jp + half], slot).then_inc(slab_done, 1)

                def down_step(j, jp, slot, first, last):
                    pe.wait_ge(low_ready, low_at(l, slab_d(j)))
                    pe.wait_ge(ff_dve, ffd(l, j, "low"))
                    row_slab(slot, gh[:, jp], gl[:, jp], first, last).then_inc(slab_done, 1)

                for t in range(TT):
                    for half, n in enumerate((slab_v(0), slab_g(0))):
                        for c in range(2):
                            waits = half == 0 and c == 0
                            ins = pass_by_pass(bank[half], n % RING, l, n, c, t * P, P,
                                               (lambda kp: f"2hi{t}{kp}1") if waits else None,
                                               (lambda kp: f"2lo{t}{kp}") if waits else None)
                            if t == 0 and half == 1 and c == 0:
                                norm_tile(l, 1)
                        if t == 1:
                            ins.then_inc(slab_done, 1)
                up_step(1, 1, slab_v(1) % RING, slab_g(1) % RING)
                pe.wait_ge(x_new, x_at(l, 4))
                down_step(0, 0, slab_d(0) % RING, True, False)
                with pe.Fori(0, (J - 3) // 2) as i:
                    up_step(i * 2 + 2, 0, slab_v(2) % RING, slab_g(2) % RING)
                    down_step(i * 2 + 1, 1, slab_d(1) % RING, False, False)
                    up_step(i * 2 + 3, 1, slab_v(3) % RING, slab_g(3) % RING)
                    down_step(i * 2 + 2, 0, slab_d(2) % RING, False, False)
                up_step(J - 1, 0, slab_v(J - 1) % RING, slab_g(J - 1) % RING)
                down_step(J - 2, 1, slab_d(J - 2) % RING, False, False)
                down_step(J - 1, 0, slab_d(J - 1) % RING, False, True)

        @block.scalar
        def _(act):
            def high(l, n, slot, raw, uses_before, done):
                act.wait_ge(slab_in[raw], l * (16 * PER_SLOT[raw]) + (uses_before + 1) * 16)
                act.wait_ge(slab_done, done)
                nc.scalar.activation(wh[:, slot, :], wf[:, raw, :], ACT.Copy, scale=WS).then_inc(high_ready, 1)

            def high_of(l, n):
                high(l, n, n % RING, n % RAW, n // RAW,
                     done_at(l, n - RING if n >= RING else last_in_slot(n, RING) - NSLAB))

            act.wait_ge(setup, 3)
            nc.scalar.activation(lbx[:, 3, :], lbx[:, 2, :], ACT.Exp).then_inc(setup_act, 1)

            def norm(l, w, extra):
                for t in range(TT):
                    for e in range(2):
                        act.wait_ge(x_new, x_at(l, 2 * t + e - 3))
                        nc.scalar.activation(xn[:, t, e * 512:(e + 1) * 512], xr[:, t, e * 512:(e + 1) * 512], ACT.Square,
                                             accum_out=ss[:, t, e:e + 1]).then_inc(nm_act.mark(f"{w}sq{t}{e}"), 1)
                for n in extra:
                    high_of(l, n)
                act.wait_ge(mixp_in, l * 16 + 16)
                for kp in range(4):
                    act.wait_ge(nm_pe.sem, nm_pe.at(l, f"{w}T{kp}"))
                    for c in range(2):
                        g = m_("g_mix", 2 * kp + c, 1)
                        nc.scalar.activation(hh[:, 2 * kp + c, :], bank_of(f"n{w}{kp}")[:, c * T:(c + 1) * T],
                                             ACT.Copy, scale=g).then_inc(nm_act.mark(f"{w}hi{kp}{c}"), 1)

            def squares(l, t):
                for e in range(2):
                    act.wait_ge(x_new, x_at(l, 2 * t + e + 1))
                    nc.scalar.activation(xn[:, t, e * 512:(e + 1) * 512], xr[:, t, e * 512:(e + 1) * 512], ACT.Square,
                                         accum_out=ss[:, t, e:e + 1]).then_inc(nm_act.mark(f"2sq{t}{e}"), 1)

            def high_tile(l, t):
                for kp in range(4):
                    if kp % 2 == 0:
                        act.wait_ge(nm_pe.sem, nm_pe.at(l, f"2T{t}{kp // 2}"))
                    for c in range(2):
                        at = (kp % 2) * 256 + c * P
                        nc.scalar.activation(hh[:, 2 * kp + c, t * P:(t + 1) * P], bank_of(f"n2{t}{kp // 2}")[:, at:at + P],
                                             ACT.Copy, scale=f_("g_ffn", 2 * kp + c, 1)).then_inc(nm_act.mark(f"2hi{t}{kp}{c}"), 1)

            with act.Fori(0, L) as l:
                norm(l, 1, [0])
                act.wait_ge(const_in, l * 16 + 16)
                for n in range(1, AHEAD):
                    high_of(l, n)

                def task(name):
                    b = bank_of(name) if name in uses else None
                    if name == "kdT":
                        act.wait_ge(hg_pe.sem, hg_pe.at(l, name))
                        for e in range(8):
                            nc.scalar.activation(kdm[:, e, :], b[:, :], ACT.Copy, scale=cst[:, CONST["blk8"][0] + e:CONST["blk8"][0] + e + 1]).then_inc(hg_act.mark(f"kdm{e}"), 1)
                    elif name == "vT":
                        act.wait_ge(hg_pe.sem, hg_pe.at(l, name))
                        nc.scalar.activation(vt[:, :, :].rearrange("p t c -> p (t c)"), b[:, :], ACT.Copy).then_inc(hg_act.mark("vt"), 1)
                    elif name.startswith("lat_q"):
                        t = int(name[-1])
                        act.wait_ge(la_pe.sem, la_pe.at(l, name))
                        act.wait_ge(la_pool.sem, la_pool.at(l, "lat_rs"))
                        nc.scalar.activation(qk[:, 4 * t:4 * t + 4, :].rearrange("p h c -> p (h c)"), b[:, 0:NH * QK], ACT.Copy,
                                             scale=lat_rs[:, t:t + 1]).then_inc(la_act.mark(f"q{t}"), 1)
                    elif name.startswith("lat_kv"):
                        t = int(name[-1])
                        act.wait_ge(la_pe.sem, la_pe.at(l, name))
                        bv = b[:, :].rearrange("p (h c) -> p h c", h=NH)
                        nc.scalar.activation(qk[:, 8 + 4 * t:12 + 4 * t, 0:NOPE], bv[:, :, 0:NOPE], ACT.Copy,
                                             scale=lat_rs[:, 2 + t:3 + t]).then_inc(la_act.mark(f"k{t}"), 1)
                        nc.scalar.activation(vm[:, t, :, :], bv[:, :, NOPE:P], ACT.Copy,
                                             scale=lat_rs[:, 2 + t:3 + t]).then_inc(la_act.mark(f"vm{t}"), 1)
                    elif name[0] == "z":
                        h = int(name[1])
                        act.wait_ge(sk_pe.sem, sk_pe.at(l, name))
                        nc.scalar.activation(beta[:, h, :], b[:, 0:384], ACT.Sigmoid).then_inc(sk_act.mark(f"beta{h}"), 1)
                        nc.scalar.activation(omb[:, h, :], b[:, 0:384], ACT.Sigmoid, scale=-1.0).then_inc(sk_act.mark(f"omb{h}"), 1)
                    elif name.startswith("qkT"):
                        u = int(name[3])
                        act.wait_ge(la_pe.sem, la_pe.at(l, name))
                        nc.scalar.activation(qkT[0:QK, u // 2, 2 * (u % 2):2 * (u % 2) + 2, :].rearrange("p h t -> p (h t)"), b[0:QK, :], ACT.Copy).then_inc(la_act.mark(name), 1)
                    elif name == "exps":
                        act.wait_ge(la_dve.sem, la_dve.at(l, "nmx"))
                        for h in range(NH):
                            for t in range(TT):
                                a, w_ = (0, P) if t == 0 else (P, T)
                                nc.scalar.activation(pr[:, h, a:a + w_], sc[:, h, a:a + w_], ACT.Exp, bias=nmx[:, t * 4 + h:t * 4 + h + 1],
                                                     scale=QK ** -0.5, accum_out=den[:, t * 4 + h:t * 4 + h + 1]).then_inc(la_act.mark(f"exp{h}{t}"), 1)
                    elif name.startswith("wT") or name.startswith("pT"):
                        h = int(name[2])
                        s_, a_s, dst = (sk_pe, sk_act, wT) if name[0] == "w" else (la_pe, la_act, prT)
                        act.wait_ge(s_.sem, s_.at(l, name))
                        nc.scalar.activation(dst[:, h, :], b[:, 0:384], ACT.Copy).then_inc(a_s.mark(name), 1)
                    elif name in ("skv", "lav"):
                        s_, a_s, i_ = (sk_pe, sk_act, 3) if name == "skv" else (la_pe, la_act, 1)
                        act.wait_ge(s_.sem, s_.at(l, name))
                        nc.scalar.activation(y32[i_], b[:, :], ACT.Copy).then_inc(a_s.mark("y"), 1)
                        act.wait_ge(a_s.sem, a_s.at(l, "y"))
                        nc.scalar.activation(yh[:, i_, :, :].rearrange("p c t -> p (c t)"), y32[i_], ACT.Copy).then_inc(a_s.mark("hi"), 1)
                    elif name == "osq":
                        act.wait_ge(hg_dve.sem, hg_dve.at(l, f"o{BW - 1}"))
                        nc.scalar.activation(osq, o[:, :, :].rearrange("p c t -> p (c t)"), ACT.Square).then_inc(hg_act.mark("osq"), 1)
                    elif name == "hgy":
                        act.wait_ge(hg_dve.sem, hg_dve.at(l, "y"))
                        nc.scalar.activation(yh[:, 0, :, :].rearrange("p c t -> p (c t)"), y32[0], ACT.Copy).then_inc(hg_act.mark("hi"), 1)
                    elif name == "lnB":
                        act.wait_ge(cv_pe.sem, cv_pe.at(l, name))
                        for c in range(2):
                            nc.scalar.activation(cz[:, c, :], b[:, c * T:(c + 1) * T], ACT.Identity, scale=m_("ln_g", c, 1), bias=m_("ln_b", c, 1)).then_inc(cv_act.mark(f"z{c}"), 1)
                        for c in range(2):
                            nc.scalar.activation(csig[:, c, :], b[:, c * T:(c + 1) * T], ACT.Sigmoid, scale=m_("ln_g", c, 1), bias=m_("ln_b", c, 1)).then_inc(cv_act.mark(f"sig{c}"), 1)
                    elif name == "cvy":
                        act.wait_ge(cv_pool.sem, cv_pool.at(l, "y"))
                        nc.scalar.activation(yh[:, 2, :, :].rearrange("p c t -> p (c t)"), y32[2], ACT.Copy).then_inc(cv_act.mark("hi"), 1)
                    else:
                        raise ValueError(name)

                tasks = {7: ["lat_q0", "lat_q1", "lat_kv0", "lat_kv1"], 8: ["kdT", "vT"],
                         15: ["z0", "z1", "z2", "z3"], 16: ["qkT0", "qkT1", "qkT2", "qkT3"],
                         18: ["exps"], 19: ["wT0", "wT1", "wT2", "wT3"], 20: ["osq"], 21: ["skv"],
                         22: ["pT0", "pT1", "pT2", "pT3"], 23: ["lav"], 24: ["hgy", "lnB"], 25: ["cvy"]}

                def whole(ap2):
                    return ap2[:, :, :].rearrange("p c t -> p (c t)")

                for n in range(S_BR):
                    high_of(l, n + AHEAD)
                    b = bank_of(f"slab{n}")
                    act.wait_ge(slab_done, done_at(l, n))
                    if n == S_HQ:
                        nc.scalar.activation(whole(q), b[:, :], ACT.Sigmoid, scale=IWS).then_inc(hg_act.mark("sig_q"), 1)
                    elif n == S_HF:
                        nc.scalar.activation(whole(f), b[:, :], ACT.Sigmoid, scale=IWS).then_inc(hg_act.mark("sf"), 1)
                        nc.scalar.activation(whole(k), b[:, :], ACT.Sigmoid, scale=-IWS).then_inc(hg_act.mark("smf"), 1)
                    elif n == S_HV:
                        nc.scalar.activation(whole(v), b[:, :], ACT.Copy, scale=IWS).then_inc(hg_act.mark("v"), 1)
                    elif n == S_HG:
                        nc.scalar.activation(whole(gg), b[:, :], ACT.Sigmoid, scale=IWS).then_inc(hg_act.mark("sig_g"), 1)
                    elif n == S_CQ:
                        nc.scalar.activation(whole(cqs), b[:, :], ACT.Square, scale=IWS).then_inc(la_act.mark("cqs"), 1)
                        act.wait_ge(la_dve.sem, la_dve.at(l, "gql"))
                        for c in range(2):
                            nc.scalar.activation(cqg[:, c, :], b[:, c * T:(c + 1) * T], ACT.Copy, scale=gql[:, c:c + 1]).then_inc(la_act.mark(f"cqg{c}"), 1)
                    elif n == S_KV:
                        nc.scalar.activation(kvs, b[:, 0:T], ACT.Square, scale=IWS).then_inc(la_act.mark("kvs"), 1)
                        nc.scalar.activation(kvg, b[:, 0:T], ACT.Copy, scale=gql[:, 2:3]).then_inc(la_act.mark("kvg"), 1)
                        nc.scalar.activation(whole(kr), b[:, T:T + TT * ROPE], ACT.Copy, scale=IWS).then_inc(la_act.mark("kr"), 1)
                    elif n == S_CA:
                        nc.scalar.activation(whole(ca), b[:, :], ACT.Copy, scale=IWS).then_inc(cv_act.mark("ca"), 1)
                    elif n == S_CG:
                        nc.scalar.activation(whole(sg_c), b[:, :], ACT.Sigmoid, scale=IWS).then_inc(cv_act.mark("sg"), 1)
                    elif n == S_SQ:
                        nc.scalar.activation(whole(sqT), b[:, :], ACT.Copy, scale=HD ** -0.5 * IWS).then_inc(sk_act.mark("sq"), 1)
                    elif n == S_SK:
                        nc.scalar.activation(whole(skT), b[:, :], ACT.Copy, scale=IWS).then_inc(sk_act.mark("sk"), 1)
                    elif n == S_SV:
                        nc.scalar.activation(whole(sv), b[:, :], ACT.Copy, scale=IWS).then_inc(sk_act.mark("sv"), 1)
                    else:
                        g = n - S_GATE
                        nc.scalar.activation(gates[:, GATE_ORDER[g // 4], 2 * (g % 4):2 * (g % 4) + 2, :].rearrange("p c t -> p (c t)"), b[:, :],
                                             ACT.Sigmoid, scale=IWS).then_inc(mg_act.mark(f"gate{g}"), 1)
                    for name in tasks.get(n, []):
                        task(name)
                for n in range(S_BR + AHEAD, S_FF):
                    high_of(l, n)
                for r in range(4):
                    act.wait_ge(mg_dve.sem, mg_dve.at(l, f"a3{r}"))
                    nc.scalar.activation(mh[:, 2 * r:2 * r + 2, :].rearrange("p c t -> p (c t)"),
                                         mg[:, 2 * r:2 * r + 2, :].rearrange("p c t -> p (c t)"), ACT.Copy).then_inc(mg_act.mark(f"hi{r}"), 1)
                for n in range(S_FF, S_FF + 2):
                    high_of(l, n)
                squares(l, 0)
                for n in range(S_FF + 2, S_FF + 4):
                    high_of(l, n)
                act.wait_ge(ffp_in, l * 16 + 16)
                high_tile(l, 0)
                squares(l, 1)
                high_tile(l, 1)
                high_of(l, S_FF + 4)

                def ff_step(j, jp):
                    for half, (u, n) in enumerate(((u_v, slab_v(j)), (u_g, slab_g(j)))):
                        act.wait_ge(slab_done, done_at(l, n))
                        if half == 0 and (not isinstance(j, int) or j >= 2):
                            act.wait_ge(ff_dve, ffd(l, j - 2, "low"))
                        for c in range(2):
                            tap, bias = tap_of(j, half, c, 2), bias_of(j, half, c)
                            nc.scalar.activation(u[:, jp, c, :], bank[2 * jp + half][:, c * T:(c + 1) * T], ACT.Identity,
                                                 scale=tap, bias=bias).then_inc(ff_act, 1)
                    act.wait_ge(ff_dve, ffd(l, j, "g1b"))
                    nc.scalar.activation(u_g[:, jp, :, :].rearrange("p c t -> p (c t)"), u_g[:, jp, :, :].rearrange("p c t -> p (c t)"), ACT.Silu).then_inc(ff_act, 1)
                    act.wait_ge(ff_dve, ffd(l, j, "mul"))
                    if not isinstance(j, int) or j >= 2:
                        act.wait_ge(slab_done, done_at(l, slab_d(j - 2)))
                    nc.scalar.activation(gh[:, jp, :, :].rearrange("p c t -> p (c t)"), u_v[:, jp, :, :].rearrange("p c t -> p (c t)"), ACT.Copy).then_inc(ff_act, 1)

                act.wait_ge(ff_tap, l + 1)
                ff_step(0, 0)
                for n in range(S_FF + 5, S_FF + 8):
                    high_of(l, n)
                ff_step(1, 1)
                with act.Fori(0, (J - 3) // 2) as i:
                    for e in range(2):
                        for m in range(3):
                            n0 = S_FF + 8 + 3 * e + m
                            high(l, None, n0 % RING, n0 % RAW, i * 2 + n0 // RAW, done_at(l, i * 6 + (n0 - RING)))
                        ff_step(i * 2 + (2 + e), e)
                high_of(l, NSLAB - 1)
                ff_step(J - 1, 0)

        @block.vector
        def _(dve):
            dve.sem_inc(mg_dve.sem, START)
            dve.sem_inc(ff_dve, START)
            dve.sem_inc(low_ready, RAW)
            dve.wait_ge(logits_in, 16)
            l0, l1 = lbx[:, 0, 0:2], lbx[:, 0, 2:4]
            nc.vector.tensor_tensor(lbx[:, 1, 0:2], l0, l1, ALU.max).then_inc(setup, 1)
            dve.wait_ge(setup, 1)
            nc.vector.tensor_tensor(lbx[:, 2, 0:2], l0, lbx[:, 1, 0:2], ALU.subtract).then_inc(setup, 1)
            nc.vector.tensor_tensor(lbx[:, 2, 2:4], l1, lbx[:, 1, 0:2], ALU.subtract).then_inc(setup, 1)
            dve.wait_ge(setup_act, 1)
            e0, e1 = lbx[:, 3, 0:2], lbx[:, 3, 2:4]
            nc.vector.tensor_tensor(lbx[:, 4, 0:2], e0, e1, ALU.add).then_inc(setup, 1)
            dve.wait_ge(setup, 4)
            nc.vector.reciprocal(lbx[:, 5, 0:2], lbx[:, 4, 0:2]).then_inc(setup, 1)
            dve.wait_ge(setup, 5)
            nc.vector.tensor_tensor(lbx[:, 6, 0:2], e0, lbx[:, 5, 0:2], ALU.mult).then_inc(setup, 1)
            nc.vector.tensor_tensor(lbx[:, 6, 2:4], e1, lbx[:, 5, 0:2], ALU.mult).then_inc(setup, 1)
            dve.wait_ge(setup, 7)
            nc.vector.tensor_tensor(lbx[:, 7, 0:2], lbx[:, 6, 0:2], lbx[:, 6, 2:4], ALU.add).then_inc(setup, 1)
            nc.vector.tensor_tensor(lbt[:, 0:2], lbx[:, 6, 0:2], lbx[:, 6, 0:2], ALU.subtract).then_inc(setup, 1)
            dve.wait_ge(setup, 9)
            nc.vector.tensor_tensor(lbt[:, 2:4], lbx[:, 7, 0:2], lbx[:, 6, 0:2], ALU.subtract).then_inc(setup, 1)
            dve.wait_ge(setup, 10)
            nc.vector.tensor_scalar(omlbt[:, :], lbt[:, :], -1.0, 1.0, ALU.mult, ALU.add).then_inc(setup, 1)
            dve.wait_ge(setup, 11)
            dve.wait_ge(x_in[0], 16)
            dve.sem_inc(x_new, 2)
            dve.wait_ge(x_in[1], 16)
            dve.sem_inc(x_new, 2)
            dve.wait_ge(pool_setup, 2)

            def TTo(out_, a, b, op):
                return nc.vector.tensor_tensor(out_, a, b, op)

            def STT(out_, a, s_, b, op0=ALU.mult, op1=ALU.add):
                return nc.vector.scalar_tensor_tensor(out=out_, in0=a, scalar=s_, in1=b, op0=op0, op1=op1)

            def own(s_, l, step):
                dve.wait_ge(s_.sem, s_.at(l, step))

            def whole(ap2):
                return ap2[:, :, :].rearrange("p c t -> p (c t)")

            with dve.Fori(0, L) as l:
                def split_at(n, slot, raw):
                    dve.wait_ge(high_ready, slab_at(l, n))
                    STT(wl[:, slot, :], wf[:, raw, :], WS, wh[:, slot, :], ALU.mult, ALU.subtract).then_inc(low_ready, 1)

                def split(n):
                    split_at(n, n % RING, n % RAW)

                def mean_square(l, w, t):
                    dve.wait_ge(nm_act.sem, nm_act.at(l, f"{w}sq{t}0"))
                    nc.vector.tensor_scalar(ms0[:, t:t + 1], ss[:, t, 0:1], 1.0 / D, EPS, ALU.mult, ALU.add).then_inc(nm_dve.mark(f"{w}ms0{t}"), 1)
                    own(nm_dve, l, f"{w}ms0{t}")
                    dve.wait_ge(nm_act.sem, nm_act.at(l, f"{w}sq{t}1"))
                    STT(ms[:, t:t + 1], ss[:, t, 1:2], 1.0 / D, ms0[:, t:t + 1]).then_inc(nm_dve.mark(f"{w}ms{t}"), 1)

                def scale_rows(l, w, t):
                    dve.wait_ge(nm_pool.sem, nm_pool.at(l, f"{w}rs{t}"))
                    for e in range(2):
                        nc.vector.tensor_scalar(xn[:, t, e * 512:(e + 1) * 512], xr[:, t, e * 512:(e + 1) * 512], rs[:, t:t + 1],
                                                None, ALU.mult).then_inc(nm_dve.mark(f"{w}xn{t}{e}"), 1)

                def norm(l, w, extra):
                    scale_rows(l, w, 0)
                    mean_square(l, w, 1)
                    scale_rows(l, w, 1)
                    for n in extra:
                        split(n)
                    dve.wait_ge(mixp_in, l * 16 + 16)
                    for kp in range(4):
                        dve.wait_ge(nm_act.sem, nm_act.at(l, f"{w}hi{kp}1"))
                        for c in range(2):
                            g = m_("g_mix", 2 * kp + c, 1)
                            ins = STT(hl[:, 2 * kp + c, :], bank_of(f"n{w}{kp}")[:, c * T:(c + 1) * T], g,
                                      hh[:, 2 * kp + c, :], ALU.mult, ALU.subtract)
                        ins.then_inc(nm_dve.mark(f"{w}lo{kp}"), 1)

                def low_of(s_, act_s, i_):
                    dve.wait_ge(act_s.sem, act_s.at(l, "hi"))
                    nc.vector.tensor_tensor(yl[:, i_, :, :].rearrange("p c t -> p (c t)"), y32[i_],
                                            yh[:, i_, :, :].rearrange("p c t -> p (c t)"), ALU.subtract).then_inc(s_.mark("lo"), 1)

                def task(name):
                    b = bank_of(name) if name in uses else None
                    if name == "q":
                        dve.wait_ge(hg_act.sem, hg_act.at(l, "sig_q"))
                        STT(whole(q), bank_of("slab0")[:, :], IWS, whole(q), ALU.mult, ALU.mult).then_inc(hg_dve.mark("q"), 1)
                    elif name == "f":
                        nc.vector.tensor_copy(lb[:, :], lbt[:, bass.ds(l * 2, 2)]).then_inc(hg_dve.mark("lb"), 1)
                        nc.vector.tensor_copy(omlb[:, :], omlbt[:, bass.ds(l * 2, 2)]).then_inc(hg_dve.mark("omlb"), 1)
                        dve.wait_ge(hg_act.sem, hg_act.at(l, "smf"))
                        own(hg_dve, l, "omlb")
                        for c in range(2):
                            nc.vector.tensor_scalar(f[:, c, :], f[:, c, :], omlb[:, c:c + 1], lb[:, c:c + 1],
                                                    ALU.mult, ALU.add).then_inc(hg_dve.mark(f"f{c}"), 1)
                        for c in range(2):
                            nc.vector.tensor_scalar(k[:, c, :], k[:, c, :], omlb[:, c:c + 1], None,
                                                    ALU.mult).then_inc(hg_dve.mark(f"k{c}"), 1)
                        own(hg_dve, l, "f1")
                        dve.wait_ge(hg_pool.sem, hg_pool.at(l, "zero"))
                        fb, ib, sb_, nb = blocks(f[:, :, :]), blocks(f_in[:, :, :]), blocks(f_first[:, :, :]), blocks(f_next[:, :, :])
                        nc.vector.tensor_copy(ib[:, :, 1:BW], fb[:, :, 1:BW]).then_inc(hg_dve.mark("f_in"), 1)
                        nc.vector.tensor_copy(sb_[:, :, 0:1], fb[:, :, 0:1]).then_inc(hg_dve.mark("f_first"), 1)
                        nc.vector.tensor_copy(nb[:, :, 0:BW - 1], fb[:, :, 1:BW]).then_inc(hg_dve.mark("f_next"), 1)
                        own(hg_dve, l, "f_next")
                        for c in range(2):
                            nc.vector.tensor_tensor_scan(pre[:, c, :], f_in[:, c, :], f_first[:, c, :], 0.0, ALU.mult, ALU.add).then_inc(hg_dve.mark(f"pre{c}"), 1)
                        for c in range(2):
                            nc.vector.tensor_tensor_scan(kd[:, c, ::-1], f_next[:, c, ::-1], c_("ends")[:, ::-1], 0.0, ALU.mult, ALU.add).then_inc(hg_dve.mark(f"suf{c}"), 1)
                        own(hg_dve, l, "suf1")
                        for e in range(2):
                            STT(whole(qdm[:, e]), whole(q), cst[:, CONST["headmask"][0] + e:CONST["headmask"][0] + e + 1], whole(pre),
                                ALU.mult, ALU.mult).then_inc(hg_dve.mark(f"qd{e}"), 1)
                    elif name == "gg":
                        dve.wait_ge(hg_act.sem, hg_act.at(l, "sig_g"))
                        STT(whole(gg), bank_of(f"slab{S_HG}")[:, :], IWS, whole(gg), ALU.mult, ALU.mult).then_inc(hg_dve.mark("gg"), 1)
                    elif name.startswith("lag"):
                        d = int(name[3:])
                        w_ = BW - d
                        n = 2 * NB * w_
                        dve.wait_ge(hg_pe.sem, hg_pe.at(l, name))
                        bv = b[:, 0:n].rearrange("p (b w) -> p b w", w=w_)
                        ob, vb = blocks(o[:, :, :]), blocks(v[:, :, :])
                        if d == 0:
                            TTo(ob, bv, vb, ALU.mult).then_inc(hg_dve.mark("t0"), 1)
                        else:
                            tv = olag[:, d % 2, 0:n].rearrange("p (b w) -> p b w", w=w_)
                            TTo(tv, bv, vb[:, :, 0:w_], ALU.mult).then_inc(hg_dve.mark(f"t{d}"), 1)
                            own(hg_dve, l, f"t{d}")
                            if 0 <= d + 4 - 1 - INTER_AT < 4:
                                own(hg_dve, l, f"oi{d + 3 - INTER_AT}1")
                            TTo(ob[:, :, d:BW], ob[:, :, d:BW], tv, ALU.add).then_inc(hg_dve.mark(f"o{d}"), 1)
                    elif name.startswith("ds"):
                        r = int(name[2:])
                        dve.wait_ge(hg_pe.sem, hg_pe.at(l, name))
                        for e in range(2):
                            bl = 2 * r + e
                            if bl == NB - 1:
                                continue
                            if bl > 0:
                                own(hg_dve, l, f"st{bl}1")
                            for c in range(2):
                                src = b[:, e * 256 + c * P:e * 256 + (c + 1) * P]
                                dst = st[:, bl + 1, c * P:(c + 1) * P]
                                if bl == 0:
                                    nc.vector.tensor_copy(dst, src).then_inc(hg_dve.mark(f"st1{c}"), 1)
                                else:
                                    STT(dst, st[:, bl, c * P:(c + 1) * P], pre[:, c, bl * BW + BW - 1:bl * BW + BW], src).then_inc(hg_dve.mark(f"st{bl + 1}{c}"), 1)
                    elif name.startswith("inter"):
                        i_ = int(name[5])
                        own(hg_dve, l, f"o{INTER_AT + i_ - 4}")
                        dve.wait_ge(hg_pe.sem, hg_pe.at(l, name))
                        b0 = 1 if i_ == 0 else 0
                        for e in range(2):
                            r0 = e * HD
                            ov = o[r0:r0 + HD, :, :].rearrange("p c (b w) -> p c b w", w=BW)[:, :, 4 * i_ + b0:4 * i_ + 4, :]
                            iv = b[r0:r0 + HD, 0:2 * P].rearrange("p (c b e w) -> p c b e w", c=2, b=4, e=2)[:, :, b0:, e, :]
                            TTo(ov, ov, iv, ALU.add).then_inc(hg_dve.mark(f"oi{i_}{e}"), 1)
                    elif name == "oss":
                        dve.wait_ge(hg_pe.sem, hg_pe.at(l, name))
                        nc.vector.tensor_scalar(o_ms[:, :], b[:, 0:8], 1.0 / HD, EPS, ALU.mult, ALU.add).then_inc(hg_dve.mark("o_ms"), 1)
                    elif name == "hgy":
                        dve.wait_ge(hg_pe.sem, hg_pe.at(l, "orT"))
                        TTo(osq, whole(o), bank_of("orT")[:, :], ALU.mult).then_inc(hg_dve.mark("on"), 1)
                        own(hg_dve, l, "on")
                        STT(osq, osq, m_("g_hg"), whole(gg), ALU.mult, ALU.mult).then_inc(hg_dve.mark("y"), 1)
                    elif name == "orx":
                        dve.wait_ge(hg_pool.sem, hg_pool.at(l, "o_rs"))
                        nc.vector.tensor_copy(orx.rearrange("p t (e d) -> p (t e) d", d=HD),
                                              o_rs[:, :].unsqueeze(2).to_broadcast([P, 8, HD])).then_inc(hg_dve.mark("orx"), 1)
                    elif name == "hglo":
                        low_of(hg_dve, hg_act, 0)
                    elif name == "lat_ms":
                        dve.wait_ge(la_pe.sem, la_pe.at(l, "lat_ss"))
                        bs = bank_of("lat_ss")
                        nc.vector.tensor_scalar(lat_ms[:, 0:2], bs[:, 0:2], 1.0 / 256, EPS, ALU.mult, ALU.add).then_inc(la_dve.mark("lat_ms0"), 1)
                        nc.vector.tensor_scalar(lat_ms[:, 2:4], bs[:, 2:4], 1.0 / 128, EPS, ALU.mult, ALU.add).then_inc(la_dve.mark("lat_ms1"), 1)
                    elif name == "qk_ms":
                        dve.wait_ge(la_pool.sem, la_pool.at(l, "qksq"))
                        nc.vector.tensor_reduce(qk_ss[:, :], qksq[:, :, :], AX.X, ALU.add).then_inc(la_dve.mark("qk_ss"), 1)
                        own(la_dve, l, "qk_ss")
                        nc.vector.tensor_scalar(qk_ms[:, :], qk_ss[:, :], 1.0 / QK, EPS, ALU.mult, ALU.add).then_inc(la_dve.mark("qk_ms"), 1)
                    elif name == "s":
                        for h in range(NH):
                            dve.wait_ge(la_pe.sem, la_pe.at(l, f"s{h}"))
                            TTo(sc[:, h, :], bank_of(f"s{h}")[:, 0:384], c_("neg"), ALU.add).then_inc(la_dve.mark(f"sc{h}"), 1)
                        own(la_dve, l, "sc3")
                        nc.vector.tensor_reduce(mx[:, 0:4], sc[:, :, 0:P], AX.X, ALU.max).then_inc(la_dve.mark("mx0"), 1)
                        nc.vector.tensor_reduce(mx[:, 4:8], sc[:, :, P:384], AX.X, ALU.max).then_inc(la_dve.mark("mx1"), 1)
                        own(la_dve, l, "mx1")
                        nc.vector.tensor_scalar(nmx, mx, -(QK ** -0.5), None, ALU.mult).then_inc(la_dve.mark("nmx"), 1)
                    elif name == "rden":
                        dve.wait_ge(la_act.sem, la_act.at(l, "exp31"))
                        nc.vector.reciprocal(rden, den).then_inc(la_dve.mark("rden"), 1)
                    elif name == "lalo":
                        low_of(la_dve, la_act, 1)
                    elif name.startswith("taps"):
                        first, count = TAPS[name]
                        for tap in range(first, first + count):
                            for c in range(2):
                                wcol = m_("conv_w", c * CK + tap, 1)
                                if tap == 0:
                                    if c == 0:
                                        dve.wait_ge(cv_pool.sem, cv_pool.at(l, "u"))
                                    nc.vector.tensor_scalar(cacc[:, c, :], cu[:, c, 0:T], wcol, m_("conv_b", c, 1), ALU.mult, ALU.add).then_inc(cv_dve.mark(f"tap0{c}"), 1)
                                else:
                                    own(cv_dve, l, f"tap{tap - 1}{c}")
                                    STT(cacc[:, c, :], cu[:, c, tap:tap + T], wcol, cacc[:, c, :]).then_inc(cv_dve.mark(f"tap{tap}{c}"), 1)
                    elif name == "ln":
                        dve.wait_ge(cv_pe.sem, cv_pe.at(l, "lnT"))
                        b = bank_of("lnT")
                        for t in range(TT):
                            nc.vector.bn_stats(bnst[:, t, :], b[:, t * 256:(t + 1) * 256]).then_inc(cv_dve.mark(f"bs{t}"), 1)
                    elif name == "aggr":
                        for t in range(TT):
                            nc.vector.bn_aggr(ln_ag[:, 2 * t:2 * t + 2], bnst[:, t, :]).then_inc(cv_dve.mark(f"ag{t}"), 1)
                        own(cv_dve, l, "ag1")
                        nc.vector.tensor_scalar(ln_ms, ln_ag[:, 1:4:2], 1e-5, None, ALU.add).then_inc(cv_dve.mark("ln_ms"), 1)
                    elif name == "cn":
                        dve.wait_ge(cv_pool.sem, cv_pool.at(l, "ln_rs"))
                        for t in range(TT):
                            nc.vector.tensor_scalar(cn[:, t, :], bank_of("lnT")[:, t * 256:(t + 1) * 256], ln_ag[:, 2 * t:2 * t + 1], ln_rs[:, t:t + 1],
                                                    ALU.subtract, ALU.mult).then_inc(cv_dve.mark(f"cn{t}"), 1)
                    elif name == "cvlo":
                        low_of(cv_dve, cv_act, 2)
                    elif name.startswith("scan"):
                        h = int(name[4])
                        dve.wait_ge(sk_act.sem, sk_act.at(l, f"omb{h}"))
                        nc.vector.tensor_tensor_scan(incl[:, h * 384:(h + 1) * 384][:, ::-1], omb[:, h, ::-1], c_("ge")[:, ::-1], 1.0,
                                                     ALU.mult, ALU.max).then_inc(sk_dve.mark(name), 1)
                    elif name == "sklo":
                        low_of(sk_dve, sk_act, 3)
                    else:
                        raise ValueError(name)

                TAPS = {f"taps{i}": (4 * i, min(4, CK - 4 * i)) for i in range(8)}
                tasks = {0: ["q"], 1: ["f"], 3: ["gg"]}

                def put(n, *names):
                    tasks.setdefault(n, []).extend(names)

                put(9, "qk_ms")
                for d in range(BW):
                    put(4 + d, f"lag{d}")
                put(7, "lat_ms")
                for i in range(4):
                    put(INTER_AT + i, f"inter{i}")
                for r in range(8):
                    put(10 + r // 2, f"ds{r}")
                for i, n in enumerate((8, 9, 14, 16, 17, 18, 19, 20)):
                    put(n, f"taps{i}")
                put(16, "scan0", "scan1", "scan2", "scan3")
                put(17, "s")
                put(19, "rden")
                put(21, "ln")
                put(22, "aggr", "cn")
                put(21, "sklo")
                put(21, "oss")
                put(23, "lalo")
                put(22, "orx")
                put(23, "hgy")
                put(24, "hglo")
                put(26, "cvlo")
                mean_square(l, 1, 0)
                norm(l, 1, [0])
                dve.wait_ge(const_in, l * 16 + 16)
                for n in range(1, AHEAD):
                    split(n)
                nc.vector.tensor_scalar(gql[:, :], m_("g_latent"), IWS, None, ALU.mult).then_inc(la_dve.mark("gql"), 1)
                for n in range(S_BR):
                    if "aggr" in tasks.get(n, []):
                        own(cv_dve, l, "bs1")
                    split(n + AHEAD)
                    for name in tasks.get(n, []):
                        task(name)
                def merged_low(r):
                    dve.wait_ge(mg_act.sem, mg_act.at(l, f"hi{r}"))
                    sl = slice(2 * r, 2 * r + 2)
                    TTo(ml[:, sl, :].rearrange("p c t -> p (c t)"), mg[:, sl, :].rearrange("p c t -> p (c t)"),
                        mh[:, sl, :].rearrange("p c t -> p (c t)"), ALU.subtract).then_inc(mg_dve.mark(f"lo{r}"), 1)

                for i, br in enumerate(BRANCH_ORDER):
                    if i != 2:
                        split(S_WO + min(i, 2))
                    for r in range(4):
                        if r < 3:
                            dve.wait_ge(mg_pe.sem, mg_pe.at(l, f"br{i}{r}"))
                        else:
                            dve.wait_ge(slab_done, done_at(l, S_BR + i))
                        gt = gates[:, br, 2 * r:2 * r + 2, :].rearrange("p c t -> p (c t)")
                        bk = bank_of(f"br{i}{r}")[:, :]
                        if i == 0:
                            dst = mg[:, 2 * r:2 * r + 2, :].rearrange("p c t -> p (c t)")
                        else:
                            dst = products[r]
                            if i > 1:
                                dve.wait_ge(mg_pool.sem, mg_pool.at(l, f"a{i - 1}{r}"))
                        if i == 0:
                            dve.wait_ge(mg_act.sem, mg_act.at(l, "gate15"))
                        STT(dst, bk, IWS, gt, ALU.mult, ALU.mult).then_inc(mg_dve.mark(f"m{i}{r}"), 1)
                        if i == 3:
                            m_r = mg[:, 2 * r:2 * r + 2, :].rearrange("p c t -> p (c t)")
                            own(mg_dve, l, f"m3{r}")
                            TTo(m_r, m_r, dst, ALU.add).then_inc(mg_dve.mark(f"a3{r}"), 1)
                            if r >= 1:
                                merged_low(r - 1)
                merged_low(3)

                def renew(t):
                    for e in range(2):
                        xs = xr[:, t, e * 512:(e + 1) * 512]
                        STT(xs, bank[4 + 2 * t + e][:, :], IWS, xs).then_inc(x_new, 1)

                def low_tile(t, kps):
                    for kp in kps:
                        if kp % 2 == 0:
                            dve.wait_ge(nm_act.sem, nm_act.at(l, f"2hi{t}{kp + 1}1"))
                        for c in range(2):
                            at = (kp % 2) * 256 + c * P
                            ins = STT(hl[:, 2 * kp + c, t * P:(t + 1) * P], bank_of(f"n2{t}{kp // 2}")[:, at:at + P],
                                      f_("g_ffn", 2 * kp + c, 1), hh[:, 2 * kp + c, t * P:(t + 1) * P], ALU.mult, ALU.subtract)
                        ins.then_inc(nm_dve.mark(f"2lo{t}{kp}"), 1)

                for n in range(S_WO + 3, S_FF + 2):
                    split(n)
                dve.wait_ge(half_done, l * 2 + 1)
                renew(0)
                mean_square(l, 2, 0)
                scale_rows(l, 2, 0)
                split(S_FF + 2)
                dve.wait_ge(ffp_in, l * 16 + 16)
                low_tile(0, range(4))
                dve.wait_ge(slab_done, done_at(l, S_WO + 3))
                renew(1)
                mean_square(l, 2, 1)
                scale_rows(l, 2, 1)
                split(S_FF + 3)
                low_tile(1, range(4))
                split(S_FF + 4)
                nc.vector.tensor_scalar(ftap[:, :], f_("w"), IWS, None, ALU.mult).then_inc(ff_tap, 1)

                def ff_step(j, jp):
                    for half, (u, nm) in enumerate(((u_v, "v"), (u_g, "g"))):
                        bk = bank[2 * jp + half]
                        for sh in (1, 2):
                            for c in range(2):
                                if sh == 1:
                                    if c == 0:
                                        dve.wait_ge(ff_act, ffa(l, j, f"{nm}1"))
                                else:
                                    dve.wait_ge(ff_dve, ffd(l, j, f"{nm}{c}a"))
                                STT(u[:, jp, c, sh:T], bk[:, c * T:(c + 1) * T - sh], tap_of(j, half, c, 2 - sh), u[:, jp, c, sh:T]).then_inc(ff_dve, 1)
                    uvf = u_v[:, jp, :, :].rearrange("p c t -> p (c t)")
                    dve.wait_ge(ff_act, ffa(l, j, "silu"))
                    dve.wait_ge(ff_dve, ffd(l, j, "g1b"))
                    TTo(uvf, u_g[:, jp, :, :].rearrange("p c t -> p (c t)"), uvf, ALU.mult).then_inc(ff_dve, 1)
                    dve.wait_ge(ff_act, ffa(l, j, "high"))
                    TTo(gl[:, jp, :, :].rearrange("p c t -> p (c t)"), uvf, gh[:, jp, :, :].rearrange("p c t -> p (c t)"),
                        ALU.subtract).then_inc(ff_dve, 1)

                ff_step(0, 0)
                for n in range(S_FF + 5, S_FF + 8):
                    split(n)
                ff_step(1, 1)
                with dve.Fori(0, (J - 3) // 2) as i:
                    for e in range(2):
                        for m in range(3):
                            n0 = S_FF + 8 + 3 * e + m
                            split_at(i * 6 + n0, n0 % RING, n0 % RAW)
                        ff_step(i * 2 + (2 + e), e)
                n_next = S_FF + 8 + 24
                assert n_next == NSLAB - 1
                split(NSLAB - 1)
                ff_step(J - 1, 0)
                dve.wait_ge(half_done, l * 2 + 2)
                renew(0)
                dve.wait_ge(slab_done, done_at(l, NSLAB - 1))
                renew(1)

        @block.gpsimd
        def _(pool):
            nc.gpsimd.memset(idle[:, :], 0.0).then_inc(pool_setup, 1)
            nc.gpsimd.memset(cu[:, :, 0:CK - 1], 0.0).then_inc(pool_setup, 1)
            pool.wait_ge(first_in, 16)

            def power(out_, in_, n):
                mh_ = c_("minushalf")
                return nc.gpsimd.tensor_tensor(out_, in_, mh_.to_broadcast([P, n]) if n > 1 else mh_, ALU.pow)

            def TTo(out_, a, b, op):
                return nc.gpsimd.tensor_tensor(out_, a, b, op)

            def whole(ap2):
                return ap2[:, :, :].rearrange("p c t -> p (c t)")

            def own(s_, l, step):
                pool.wait_ge(s_.sem, s_.at(l, step))

            with pool.Fori(0, L) as l:
                def rsqrt_norm(w):
                    for t in range(TT):
                        pool.wait_ge(nm_dve.sem, nm_dve.at(l, f"{w}ms{t}"))
                        power(rs[:, t:t + 1], ms[:, t:t + 1], 1).then_inc(nm_pool.mark(f"{w}rs{t}"), 1)

                def lag(d):
                    w_ = BW - d
                    n = 2 * NB * w_
                    qb, kb, fb, wb = (blocks(t_[:, :, :]) for t_ in (q, k, f, wlag))
                    if d == 1:
                        TTo(wb[:, :, 1:BW], qb[:, :, 1:BW], fb[:, :, 1:BW], ALU.mult).then_inc(hg_pool.mark("w1"), 1)
                    elif d > 1:
                        own(hg_pool, l, f"p{d - 1}")
                        TTo(wb[:, :, d:BW], wb[:, :, d:BW], fb[:, :, 1:BW - d + 1], ALU.mult).then_inc(hg_pool.mark(f"w{d}"), 1)
                    if d >= 1:
                        own(hg_pool, l, f"w{d}")
                    if d >= 2:
                        pool.wait_ge(hg_pe.sem, hg_pe.at(l, f"lag{d - 2}"))
                    src = qb if d == 0 else wb
                    TTo(plag[:, d % 2, 0:n].rearrange("p (b w) -> p b w", w=w_), src[:, :, d:BW], kb[:, :, 0:w_],
                        ALU.mult).then_inc(hg_pool.mark(f"p{d}"), 1)

                rsqrt_norm(1)
                nc.gpsimd.memset(view(g0, 0, 1536), 0.0).then_inc(hg_pool.mark("zero"), 1)
                pool.wait_ge(const_in, l * 16 + 16)
                pool.wait_ge(hg_dve.sem, hg_dve.at(l, "suf1"))
                TTo(whole(kd), whole(k), whole(kd), ALU.mult).then_inc(hg_pool.mark("kd"), 1)
                lag(0)
                lag(1)
                lag(2)
                lag(3)
                pool.wait_ge(la_act.sem, la_act.at(l, "kr"))
                qk4 = qk[:, :, :].rearrange("p (a t h) c -> p a t h c", a=2, t=TT)
                pool.wait_ge(la_dve.sem, la_dve.at(l, "lat_ms1"))
                power(lat_rs, lat_ms, 4).then_inc(la_pool.mark("lat_rs"), 1)
                lag(4)
                pool.wait_ge(cv_act.sem, cv_act.at(l, "sg"))
                TTo(cu[:, :, CK - 1:], ca[:, :, :], sg_c[:, :, :], ALU.mult).then_inc(cv_pool.mark("u"), 1)
                for t in range(TT):
                    nc.gpsimd.tensor_copy(qk4[:, 1, t, :, NOPE:QK], kr[:, t:t + 1, :].to_broadcast([P, NH, ROPE])).then_inc(la_pool.mark(f"kr{t}"), 1)
                lag(5)
                pool.wait_ge(la_act.sem, la_act.at(l, "vm1"))
                own(la_pool, l, "kr1")
                TTo(whole(qksq), whole(qk), whole(qk), ALU.mult).then_inc(la_pool.mark("qksq"), 1)
                lag(6)
                pool.wait_ge(la_dve.sem, la_dve.at(l, "qk_ms"))
                power(qk_rs[:, :], qk_ms[:, :], 16).then_inc(la_pool.mark("qk_rs"), 1)
                own(la_pool, l, "qk_rs")
                TTo(qk[:, :, :], qk[:, :, :], qk_rs[:, :].unsqueeze(2).to_broadcast([P, 16, QK]), ALU.mult).then_inc(la_pool.mark("qkn"), 1)
                own(la_pool, l, "qkn")
                lag(7)
                for a in range(2):
                    TTo(qk[:, 8 * a:8 * a + 8, :], qk[:, 8 * a:8 * a + 8, :], m_("g_qk", a * QK, QK).unsqueeze(1).to_broadcast([P, 8, QK]),
                        ALU.mult).then_inc(la_pool.mark(f"qkg{a}"), 1)
                lag(8)
                own(la_pool, l, "qkg1")
                x1, x2 = qk[:, :, NOPE:NOPE + 16], qk[:, :, NOPE + 16:QK]
                for a in range(2):
                    half = slice(8 * a, 8 * a + 8)
                    for i_, (x_, tab) in enumerate(((x1, "cos"), (x2, "sin"), (x2, "cos"), (x1, "sin"))):
                        tv = c_(tab).rearrange("p (t r) -> p t r", t=TT).unsqueeze(2).to_broadcast([P, TT, NH, 16])
                        TTo(rt[:, i_, half, :].rearrange("p (t h) r -> p t h r", t=TT), x_[:, half, :].rearrange("p (t h) r -> p t h r", t=TT),
                            tv, ALU.mult).then_inc(la_pool.mark(f"rot_{a}{i_}"), 1)
                own(la_pool, l, "rot_13")
                TTo(x1, rt[:, 0, :, :], rt[:, 1, :, :], ALU.subtract).then_inc(la_pool.mark("rot2"), 1)
                TTo(x2, rt[:, 2, :, :], rt[:, 3, :, :], ALU.add).then_inc(la_pool.mark("rot3"), 1)
                for d in range(9, 13):
                    lag(d)
                pool.wait_ge(sk_act.sem, sk_act.at(l, "omb3"))
                lag(13)
                nc.gpsimd.memset(incl[:, NH * 384:NH * 384 + 1], 1.0).then_inc(sk_pool.mark("end"), 1)
                own(sk_pool, l, "end")
                lag(14)
                pool.wait_ge(sk_dve.sem, sk_dve.at(l, "scan3"))
                TTo(whole(beta), whole(beta), incl[:, 1:NH * 384 + 1], ALU.mult).then_inc(sk_pool.mark("w1"), 1)
                own(sk_pool, l, "w1")
                TTo(beta[:, :, :], beta[:, :, :], c_("lt").unsqueeze(1).to_broadcast([P, NH, 384]), ALU.mult).then_inc(sk_pool.mark("w2"), 1)
                lag(15)
                pool.wait_ge(la_dve.sem, la_dve.at(l, "rden"))
                TTo(pr[:, :, 0:P], pr[:, :, 0:P], rden[:, 0:4].unsqueeze(2).to_broadcast([P, NH, P]), ALU.mult).then_inc(la_pool.mark("pn0"), 1)
                TTo(pr[:, :, P:384], pr[:, :, P:384], rden[:, 4:8].unsqueeze(2).to_broadcast([P, NH, T]), ALU.mult).then_inc(la_pool.mark("pn1"), 1)
                pool.wait_ge(cv_dve.sem, cv_dve.at(l, "ln_ms"))
                power(ln_rs, ln_ms, 2).then_inc(cv_pool.mark("ln_rs"), 1)
                pool.wait_ge(hg_dve.sem, hg_dve.at(l, "o_ms"))
                power(o_rs[:, :], o_ms[:, :], 8).then_inc(hg_pool.mark("o_rs"), 1)
                pool.wait_ge(cv_act.sem, cv_act.at(l, "sig1"))
                TTo(y32[2], whole(cz), whole(csig), ALU.mult).then_inc(cv_pool.mark("y"), 1)
                for i in range(1, 3):
                    for r in range(4):
                        pool.wait_ge(mg_dve.sem, mg_dve.at(l, f"m{i}{r}"))
                        if i >= 2:
                            own(mg_pool, l, f"a{i - 1}{r}")
                        d_ = mg[:, 2 * r:2 * r + 2, :].rearrange("p c t -> p (c t)")
                        TTo(d_, d_, products[r], ALU.add).then_inc(mg_pool.mark(f"a{i}{r}"), 1)
                rsqrt_norm(2)


def last_in_slot(slot, slots):
    return max(n for n in range(NSLAB) if n % slots == slot)


PER_SLOT = [sum(1 for n in range(NSLAB) if n % RAW == s) for s in range(RAW)]


def constants():
    c = np.zeros((P, NCONST), np.float32)
    p = np.arange(P)

    def put(name, a):
        c[:, CONST[name][0]:CONST[name][1]] = a

    put("ident", np.eye(P))
    put("headones", (p[:, None] // HD) == (p[None, :] // HD))
    put("blk8", (p[:, None] // BW) == np.arange(8)[None, :])
    put("ends", np.broadcast_to(np.arange(T) % BW == BW - 1, (P, T)))
    put("headmask", (p[:, None] // HD) == np.arange(2)[None, :])
    below = np.concatenate([p[None, :] < p[:, None], np.ones((P, P), bool), p[None, :] < p[:, None]], 1)
    upto = np.concatenate([p[None, :] <= p[:, None], np.ones((P, P), bool), p[None, :] <= p[:, None]], 1)
    put("neg", np.where(upto, 0.0, -1e30))
    put("ge", ~below)
    put("lt", below)
    half = ROPE // 2
    freqs = (np.float32(10000.0) ** (-np.arange(half, dtype=np.float32) / np.float32(half))).astype(np.float32)
    ang = (np.arange(T, dtype=np.float32)[:, None] * freqs[None, :]).astype(np.float32)
    for name, fn in (("cos", np.cos), ("sin", np.sin)):
        tab = fn(ang).astype(np.float32).reshape(TT, P, half).transpose(1, 0, 2)
        put(name, tab.reshape(P, -1))
    put("one", 1.0)
    put("minushalf", -0.5)
    return c


def lay_out(a):
    slabs = np.zeros((L, NSLAB, P, SLAB), np.float32)

    def cols(w, c0, n):
        s = np.zeros((P, KT, 256), np.float32)
        s[:, :, :n] = w[:, c0:c0 + n].reshape(KT, P, n).transpose(1, 0, 2)
        return s.reshape(P, SLAB)

    def rows(w, r0):
        return w[r0:r0 + 256].reshape(2, P, D).transpose(1, 0, 2).reshape(P, SLAB)

    for l in range(L):
        for n, (c0, w) in enumerate(PROJ):
            slabs[l, n] = cols(a["w_in"][l], c0, w)
        for g in range(16):
            slabs[l, S_GATE + g] = cols(a["w_in"][l], GATE0 + GATE_ORDER[g // 4] * D + (g % 4) * 256, 256)
        for i, br in enumerate(BRANCH_ORDER):
            slabs[l, S_BR + i] = rows(a["w_branch"][l, br], 0)
        for s in range(4):
            slabs[l, S_WO + s] = rows(a["w_out"][l], 256 * s)
        for j in range(J):
            slabs[l, slab_v(j)] = cols(a["w_up"][l], 256 * j, 256)
            slabs[l, slab_g(j)] = cols(a["w_up"][l], FF + 256 * j, 256)
            slabs[l, slab_d(j)] = rows(a["w_down"][l], 256 * j)

    def per_tile(v, n):
        return v.reshape(n, P).T

    mp = np.zeros((L, P, NMIXP), np.float32)
    fp = np.zeros((L, P, NFFP), np.float32)
    wup = np.zeros((L, P, NWU), np.float32)
    for l in range(L):
        def put(name, v):
            mp[l, :, MIXP[name][0]:MIXP[name][1]] = v
        put("g_mix", per_tile(a["g_mix"][l], KT))
        put("g_hg", np.concatenate([a["g_hg_out"][l]] * 2)[:, None])
        put("g_latent", np.concatenate([per_tile(a["g_q_lat"][l], 2), per_tile(a["g_kv_lat"][l], 1)], 1))
        put("g_qk", np.broadcast_to(np.concatenate([a["g_qk_q"][l], a["g_qk_k"][l]])[None], (P, 2 * QK)))
        put("conv_w", a["conv_w"][l].reshape(CK, 2, P).transpose(2, 1, 0).reshape(P, -1))
        put("conv_b", per_tile(a["conv_b"][l], 2))
        put("ln_g", per_tile(a["conv_ln_g"][l], 2))
        put("ln_b", per_tile(a["conv_ln_b"][l], 2))
        wup[l] = np.concatenate([a["w_uq"][l].reshape(2, P, NH * QK).transpose(1, 0, 2).reshape(P, -1), a["w_ukv"][l]], 1)

        def putf(name, v):
            fp[l, :, FFP[name][0]:FFP[name][1]] = v
        putf("g_ffn", per_tile(a["g_ffn"][l], KT))
        putf("w", a["ffn_conv_w"][l].reshape(3, 2, J, 2, P).transpose(4, 2, 1, 3, 0).reshape(P, -1))
        putf("b", a["ffn_conv_b"][l].reshape(2, J, 2, P).transpose(3, 1, 0, 2).reshape(P, -1))
    lbl = a["lb_logits"].reshape(L, 2, P).transpose(2, 0, 1).reshape(P, 2 * L)
    return {"x": np.ascontiguousarray(a["x"][0]), "slabs": slabs, "lb_logits": np.ascontiguousarray(lbl),
            "consts": constants(), "mixp": mp, "wup": wup, "ffp": fp}


def kernel(**inputs):
    import concourse.bacc as bacc
    from concourse.bass_utils import run_bass_kernel_spmd

    arrays = lay_out({n: np.asarray(v) for n, v in inputs.items()})
    book = {}
    for _ in range(2):
        nc = bacc.Bacc("TRN2", target_bir_lowering=False, num_devices=1)
        args = [nc.dram_tensor(f"in_{n}", v.shape, mybir.dt.from_np(v.dtype), kind="ExternalInput").ap() for n, v in arrays.items()]
        args.append(nc.dram_tensor("out_0", (T, D), mybir.dt.float32, kind="ExternalOutput").ap())
        program(nc, book, *args)
    r = run_bass_kernel_spmd(nc, [{f"in_{n}": v for n, v in arrays.items()}], core_ids=[0])
    return r.results[0]["out_0"].reshape(1, T, D)
```
